# Optimizing a Trainium2 kernel written in Bass

```python
import jax, jax.numpy as jnp
from jax import lax
import numpy as np

D_MODEL = 2048
BATCH = 1
SEQ = 256
DEPTH = 1

FOX_HEADS = 8
FOX_HEAD_DIM = 128
FOX_WIDTH = FOX_HEADS * FOX_HEAD_DIM
SWA_Q_HEADS = 16
SWA_KV_HEADS = 2
SWA_HEAD_DIM = 64
SWA_WIDTH = SWA_Q_HEADS * SWA_HEAD_DIM
SWA_KV_WIDTH = SWA_KV_HEADS * SWA_HEAD_DIM
WINDOW = 128
Q_BLOCK = 128
ROPE_THETA = 10000.0
PLE_DIM = 256
NORM_EPS = 1e-6

SPLIT_SIZES = (
    FOX_WIDTH,
    FOX_WIDTH,
    FOX_WIDTH,
    FOX_WIDTH,
    FOX_HEADS,
    SWA_WIDTH,
    SWA_KV_WIDTH,
    SWA_KV_WIDTH,
    SWA_WIDTH,
    D_MODEL,
    D_MODEL,
)
N_IN = sum(SPLIT_SIZES)

kernel_name = "fox_swa_sink_gated_hybrid"

def rms_norm(x, g):
    xf = x.astype(jnp.float32)
    y = xf * lax.rsqrt(jnp.mean(xf * xf, axis=-1, keepdims=True) + NORM_EPS)
    return (y * g.astype(jnp.float32)).astype(x.dtype)

def apply_rope(x, pos):
    half = x.shape[-1] // 2
    inv = ROPE_THETA ** (-jnp.arange(half, dtype=jnp.float32) / half)
    ang = pos.astype(jnp.float32)[..., None] * inv
    cos = jnp.cos(ang)[:, :, None, :]
    sin = jnp.sin(ang)[:, :, None, :]
    xf = x.astype(jnp.float32)
    x1, x2 = xf[..., :half], xf[..., half:]
    out = jnp.concatenate([x1 * cos - x2 * sin, x2 * cos + x1 * sin], axis=-1)
    return out.astype(x.dtype)

def forgetting_attention(q, k, v, log_f):
    B, S, H, D = q.shape
    nb = S // Q_BLOCK
    c = jnp.cumsum(log_f.astype(jnp.float32), axis=1)
    cT = c.transpose(0, 2, 1)
    qb = q.reshape(B, nb, Q_BLOCK, H, D).transpose(1, 0, 2, 3, 4)
    cb = cT.reshape(B, H, nb, Q_BLOCK).transpose(2, 0, 1, 3)
    kpos = jnp.arange(S)
    scale = D ** -0.5

    def one_block(args):
        i, q_i, c_i = args
        s = jnp.einsum('bqhd,bkhd->bhqk', q_i, k, preferred_element_type=jnp.float32) * scale
        s = s + c_i[..., :, None] - cT[..., None, :]
        qpos = i * Q_BLOCK + jnp.arange(Q_BLOCK)
        causal = kpos[None, :] <= qpos[:, None]
        s = jnp.where(causal, s, -jnp.inf)
        w = jax.nn.softmax(s, axis=-1)
        return jnp.einsum('bhqk,bkhd->bqhd', w.astype(v.dtype), v)

    out = lax.map(one_block, (jnp.arange(nb), qb, cb))
    return out.transpose(1, 0, 2, 3, 4).reshape(B, S, H, D)

def sliding_window_sink_attention(q, k, v, sinks):
    B, S, Hq, D = q.shape
    Hkv = k.shape[2]
    G = Hq // Hkv
    nb = S // WINDOW
    qb = q.reshape(B, nb, WINDOW, Hkv, G, D)
    kb = k.reshape(B, nb, WINDOW, Hkv, D)
    vb = v.reshape(B, nb, WINDOW, Hkv, D)
    pad = ((0, 0), (1, 0), (0, 0), (0, 0), (0, 0))
    kk = jnp.concatenate([jnp.pad(kb, pad)[:, :-1], kb], axis=2)
    vv = jnp.concatenate([jnp.pad(vb, pad)[:, :-1], vb], axis=2)
    s = jnp.einsum('bnqhgd,bnkhd->bnhgqk', qb, kk,
                   preferred_element_type=jnp.float32) * (D ** -0.5)
    qi = jnp.arange(WINDOW)[:, None] + WINDOW
    ki = jnp.arange(2 * WINDOW)[None, :]
    rel = qi - ki
    band = (rel >= 0) & (rel < WINDOW)
    has_prev = (jnp.arange(nb) > 0)[:, None, None] | (ki >= WINDOW)[None]
    mask = band[None] & has_prev
    s = jnp.where(mask[None, :, None, None], s, -jnp.inf)
    sink = sinks.astype(jnp.float32).reshape(Hkv, G)[None, None, :, :, None, None]
    m = jnp.maximum(jnp.max(s, axis=-1, keepdims=True), sink)
    e = jnp.exp(s - m)
    w = e / (jnp.sum(e, axis=-1, keepdims=True) + jnp.exp(sink - m))
    out = jnp.einsum('bnhgqk,bnkhd->bnqhgd', w.astype(v.dtype), vv)
    return out.reshape(B, S, Hq, D)

def setup_inputs(seed: int = 0) -> dict:
    key = jax.random.key(seed)
    ks = jax.random.split(key, 16)
    f32 = jnp.float32
    x = jax.random.normal(ks[0], (BATCH, SEQ, D_MODEL), f32)
    p = jax.random.normal(ks[1], (DEPTH, BATCH, SEQ, PLE_DIM), f32)
    offset = jax.random.randint(ks[2], (BATCH, 1), 0, 1024, dtype=jnp.int32)
    positions = (offset + jnp.arange(SEQ, dtype=jnp.int32)[None, :]).astype(jnp.int32)
    pre_norm_g = 1.0 + 0.05 * jax.random.normal(ks[3], (DEPTH, D_MODEL), f32)
    w_in = jax.random.normal(ks[4], (DEPTH, D_MODEL, N_IN), f32) * D_MODEL ** -0.5
    b_forget = jax.random.uniform(ks[5], (DEPTH, FOX_HEADS), f32, 1.0, 4.0)
    sinks = 0.5 * jax.random.normal(ks[6], (DEPTH, SWA_Q_HEADS), f32)
    w_o_fox = jax.random.normal(ks[7], (DEPTH, FOX_WIDTH, D_MODEL), f32) * FOX_WIDTH ** -0.5
    w_o_swa = jax.random.normal(ks[8], (DEPTH, SWA_WIDTH, D_MODEL), f32) * SWA_WIDTH ** -0.5
    w_out = jax.random.normal(ks[9], (DEPTH, D_MODEL, D_MODEL), f32) * D_MODEL ** -0.5
    post_norm_g = 1.0 + 0.05 * jax.random.normal(ks[10], (DEPTH, D_MODEL), f32)
    w_ple = jax.random.normal(ks[11], (DEPTH, PLE_DIM, D_MODEL), f32) * PLE_DIM ** -0.5
    w_ple_gate = jax.random.normal(ks[12], (DEPTH, D_MODEL, D_MODEL), f32) * D_MODEL ** -0.5
    return {"x": x, "p": p, "positions": positions, "pre_norm_g": pre_norm_g, "w_in": w_in,
            "b_forget": b_forget, "sinks": sinks, "w_o_fox": w_o_fox, "w_o_swa": w_o_swa,
            "w_out": w_out, "post_norm_g": post_norm_g, "w_ple": w_ple, "w_ple_gate": w_ple_gate}

def reference(x, p, positions, pre_norm_g, w_in, b_forget, sinks, w_o_fox, w_o_swa,
              w_out, post_norm_g, w_ple, w_ple_gate):
    B, S, _ = x.shape
    cuts = np.cumsum(SPLIT_SIZES)[:-1].tolist()
    for i in range(DEPTH):
        h = rms_norm(x, pre_norm_g[i])
        proj = jnp.einsum('bsd,dn->bsn', h, w_in[i])
        (q_a, k_a, v_a, z_a, f_a, q_b, k_b, v_b, z_b, g_a, g_b) = jnp.split(proj, cuts, axis=-1)

        log_f = jax.nn.log_sigmoid(f_a.astype(jnp.float32) + b_forget[i].astype(jnp.float32))
        y_a = forgetting_attention(q_a.reshape(B, S, FOX_HEADS, FOX_HEAD_DIM),
                                   k_a.reshape(B, S, FOX_HEADS, FOX_HEAD_DIM),
                                   v_a.reshape(B, S, FOX_HEADS, FOX_HEAD_DIM), log_f)
        y_a = y_a.reshape(B, S, FOX_WIDTH) * jax.nn.silu(z_a)
        y_a = jnp.einsum('bsc,cd->bsd', y_a, w_o_fox[i])

        qr = apply_rope(q_b.reshape(B, S, SWA_Q_HEADS, SWA_HEAD_DIM), positions)
        kr = apply_rope(k_b.reshape(B, S, SWA_KV_HEADS, SWA_HEAD_DIM), positions)
        y_b = sliding_window_sink_attention(qr, kr, v_b.reshape(B, S, SWA_KV_HEADS, SWA_HEAD_DIM),
                                            sinks[i])
        y_b = y_b.reshape(B, S, SWA_WIDTH) * jax.nn.silu(z_b)
        y_b = jnp.einsum('bsc,cd->bsd', y_b, w_o_swa[i])

        merged = jax.nn.sigmoid(g_a) * y_a + jax.nn.sigmoid(g_b) * y_b
        out = jnp.einsum('bsd,de->bse', merged, w_out[i])
        x = x + rms_norm(out, post_norm_g[i])

        e = jnp.einsum('bsp,pd->bsd', p[i].astype(x.dtype), w_ple[i])
        gate = jax.nn.sigmoid(jnp.einsum('bsd,de->bse', x, w_ple_gate[i]))
        x = x + gate * e
    return x


_drawn_inputs = setup_inputs


def setup_inputs(seed=0):
    import zlib

    import numpy as np

    out = dict(_drawn_inputs(seed))
    spreads = {}
    factors = {'sinks': 6.554}
    for name, (base, spread) in spreads.items():
        noise = np.random.default_rng([zlib.crc32(name.encode()), seed]).standard_normal(out[name].shape)
        drawn = base * np.exp(spread * noise) if base else spread * noise
        out[name] = __import__('jax').numpy.asarray(drawn.astype(out[name].dtype))
    for name, factor in factors.items():
        out[name] = (out[name] * factor).astype(out[name].dtype)
    return out
```

```python
from contextlib import ExitStack

import numpy as np

import concourse.bass as bass
from concourse import mybir

F32 = mybir.dt.float32
F32R = mybir.dt.float32r
I32 = mybir.dt.int32
ACT = mybir.ActivationFunctionType
ALU = mybir.AluOpType
AX = mybir.AxisListType

P = 128
D_MODEL, SEQ = 2048, 256
FOX_HEADS, FOX_DIM = 8, 128
FOX_WIDTH = FOX_HEADS * FOX_DIM
SWA_HEADS, SWA_KV, SWA_DIM = 16, 2, 64
SWA_WIDTH = SWA_HEADS * SWA_DIM
KV_WIDTH = SWA_KV * SWA_DIM
GROUP = SWA_HEADS // SWA_KV
PLE_DIM = 256
EPS = 1e-6
ROPE_THETA = 10000.0
HALF = SWA_DIM // 2
MASKED = -1e30

NT = SEQ // P
KT = D_MODEL // P
N = 512
UK = 2
RING = 4
NC = D_MODEL // N
UPC = KT // UK
UPO = FOX_WIDTH // P // UK

_SIZES = (FOX_WIDTH,) * 4 + (FOX_HEADS, SWA_WIDTH, KV_WIDTH, KV_WIDTH, SWA_WIDTH, D_MODEL, D_MODEL)
C_QA, C_KA, C_VA, C_ZA, C_F, C_QB, C_KB, C_VB, C_ZB, C_GA, C_GB = np.cumsum((0,) + _SIZES[:-1]).tolist()
KVF = 2 * KV_WIDTH + FOX_HEADS

CHUNKS = [("kvf", 0, C_KB), ("qb", 0, C_QB), ("qb", 1, C_QB + N), ("zb", 0, C_ZB), ("zb", 1, C_ZB + N)]
for _g in range(2):
    CHUNKS += [("qa", _g, C_QA + _g * N), ("ka", _g, C_KA + _g * N),
               ("va", _g, C_VA + _g * N), ("za", _g, C_ZA + _g * N)]
NCH = len(CHUNKS)

U_MIX = NCH * UPC
MIX_UNITS = 2 * UPC + 2 * UPO
E0, E1 = 1, NC - 1
U_E0 = U_MIX + NC * MIX_UNITS
U_OUT = U_E0 + E0
U_E1 = U_OUT + NC * UPC
U_GATE = U_E1 + E1
U_END = U_GATE + NC * UPC
G_MIX = NCH
G_E0 = G_MIX + 4 * NC
G_OUT = G_E0 + E0
G_E1 = G_OUT + NC
G_GATE = G_E1 + E1

HEADS = SWA_HEADS + FOX_HEADS
SCORES_AT = [5 * UPC + 2 * h for h in range(SWA_HEADS)] + [72, 76, 80, 84, 101, 103, 105, 107]
HEAD_AT = {u: h for h, u in enumerate(SCORES_AT)}
DECAY_AT = 14
BIAS_AT = 22

T_USES = [(12, "kbT", 0), (20, "qbT", 0), (21, "qbT", 1), (28, "qbT", 2), (29, "qbT", 3), (31, "pT", 0),
          (49, "qaT", 0), (50, "qaT", 1), (57, "kaT", 0), (58, "kaT", 1),
          (81, "qaT", 2), (82, "qaT", 3), (89, "kaT", 2), (90, "kaT", 3)]
T_USES += [(u + 2, "probs", h) for h, u in enumerate(SCORES_AT)]
T_USES += [(SCORES_AT[2 * q + 1] + 5, "y", q) for q in range(SWA_HEADS // 2)]
T_USES += [(SCORES_AT[SWA_HEADS + q] + 5, "y", SWA_HEADS // 2 + q) for q in range(FOX_HEADS)]
T_USES.sort(key=lambda use: use[0])
T_INDEX = {use[1:]: i for i, use in enumerate(T_USES)}
T_AT = {}
for _u in T_USES:
    T_AT.setdefault(_u[0], []).append(_u[1:])
T_MIX = len(T_USES)
T_XN = T_MIX + 2 * NC

TWO_PI_1 = 6.28125
TWO_PI_2 = float(np.float32(np.float16(2 * np.pi - TWO_PI_1)))
TWO_PI_3 = float(np.float32(2 * np.pi - TWO_PI_1 - TWO_PI_2))
ROUND = 12582912.0
PI_BELOW = 3.1415925


def build(nc, x, p, positions, pre_norm_g, w_in, b_forget, sinks, w_o_fox, w_o_swa, w_out, post_norm_g,
          w_ple, w_ple_gate, inv_freq, out):
    ctx = ExitStack()

    def sb(name, shape, dt=F32, stack=ctx):
        return stack.enter_context(nc.sbuf_tensor(name, shape, dt))

    def sem(name):
        return ctx.enter_context(nc.semaphore(name))

    with ctx:
        w_st = sb("w_st", [P, RING, UK, N])
        w_hi = sb("w_hi", [P, RING, UK, N], F32R)
        w_lo = sb("w_lo", [P, RING, UK, N], F32R)
        hT_hi = sb("hT_hi", [P, KT, SEQ], F32R)
        hT_lo = sb("hT_lo", [P, KT, SEQ], F32R)
        ident = sb("ident", [P, P])
        pT_hi = sb("pT_hi", [P, 2, SEQ], F32R)
        pT_lo = sb("pT_lo", [P, 2, SEQ], F32R)
        g1T = sb("g1T", [P, KT])
        sumsq = sb("sumsq", [P, NT])
        rms = sb("rms", [P, 5, NT])
        sumsq2 = sb("sumsq2", [P, NC, NT])
        rms2 = sb("rms2", [P, 3, NT])

        with ExitStack() as early:
            x_in = sb("x_in", [P, NT, D_MODEL], stack=early)
            p_in = sb("p_in", [P, NT, PLE_DIM], stack=early)
        with ExitStack() as late:
            x_res = sb("x_res", [P, NT, D_MODEL], stack=late)
            x_new = sb("x_new", [P, NT, D_MODEL], stack=late)
        yT_hi = sb("yT_hi", [P, 16, SEQ], F32R)
        yT_lo = sb("yT_lo", [P, 16, SEQ], F32R)

        with ExitStack() as att:
            qaT = sb("qaT", [P, FOX_HEADS, SEQ], stack=att)
            kaT = sb("kaT", [P, FOX_HEADS, SEQ], stack=att)
            qbT = sb("qbT", [P, SWA_HEADS // 2, SEQ], stack=att)
            kbT = sb("kbT", [P, SWA_KV, SEQ], stack=att)
            va = sb("va", [P, NT, FOX_WIDTH], stack=att)
            vb = sb("vb", [P, NT, KV_WIDTH], stack=att)
            sza = sb("sza", [P, NT, FOX_WIDTH], stack=att)
            szb = sb("szb", [P, NT, SWA_WIDTH], stack=att)
            bias = sb("bias", [P, FOX_HEADS, 3 * P], stack=att)
            mask = sb("mask", [P, 2, 3 * P], stack=att)
            tri = sb("tri", [P, 3 * P], stack=att)
            probs = sb("probs", [P, 2, 3 * P], stack=att)
            probsT = sb("probsT", [P, 2, 3 * P], stack=att)
            ybuf = sb("ybuf", [P, 2, NT, P], stack=att)
            raw = sb("raw", [P, NT, N], stack=att)
            rot = sb("rot", [P, NT, N], stack=att)
            rtmp = sb("rtmp", [P, NT, N], stack=att)
            trig = sb("trig", [P, 3, NT, HALF], stack=att)
            turn = sb("turn", [P, 2, NT, HALF], stack=att)
            ang = sb("ang", [P, 2, NT, HALF], stack=att)
            inv_sb = sb("inv_sb", [P, HALF], stack=att)
            pos_i = sb("pos_i", [P, NT], I32, stack=att)
            pos_f = sb("pos_f", [P, NT], stack=att)
            bf_sb = sb("bf_sb", [P, FOX_HEADS], stack=att)
            sink_sb = sb("sink_sb", [P, SWA_HEADS], stack=att)
            fg = sb("fg", [P, 4, NT, FOX_HEADS], stack=att)
            log_f = sb("log_f", [P, NT, FOX_HEADS], stack=att)
            row = sb("row", [P, 6, HEADS, NT], stack=att)
        sg = sb("sg", [P, 2, NT, N])
        mT_hi = sb("mT_hi", [P, KT, SEQ], F32R)
        mT_lo = sb("mT_lo", [P, KT, SEQ], F32R)
        ple = sb("ple", [P, NT, D_MODEL])
        g2_sb = sb("g2_sb", [P, D_MODEL])

        decay_rows = probsT[0:FOX_HEADS, 0, :]

        acc = [ctx.enter_context(nc.psum_tensor(f"acc{i}", [P, NT, N], F32)) for i in range(2)]
        tp = [ctx.enter_context(nc.psum_tensor(f"tp{i}", [P, N], F32)) for i in range(2)]
        sc = ctx.enter_context(nc.psum_tensor("sc", [P, N], F32))
        ov = ctx.enter_context(nc.psum_tensor("ov", [P, N], F32))
        four = [tp[0], tp[1], sc, ov]

        w_loaded = [sem(f"w_loaded{i}") for i in range(RING)]
        hi_ready, lo_ready, unit_done = sem("hi_ready"), sem("lo_ready"), sem("unit_done")
        acc_out = [sem("acc_out0"), sem("acc_out1")]
        t_done = sem("t_done")
        t_out = [sem("t_out0"), sem("t_out1")]
        x_loaded = [sem(f"x_loaded{i}") for i in range(4)]
        g1_loaded, pos_loaded, small_loaded, p_loaded = sem("g1_loaded"), sem("pos_loaded"), sem("small_loaded"), sem("p_loaded")
        late_loaded = [sem("x_res_loaded"), sem("g2_loaded")]
        ident_ready, masks_ready, const_ready = sem("ident_ready"), sem("masks_ready"), sem("const_ready")
        xT_done, hT_hi_ready, hT_ready = sem("xT_done"), sem("hT_hi_ready"), sem("hT_ready")
        sumsq_ready, ms_ready, pow_ready, r_ready = sem("sumsq_ready"), sem("ms_ready"), sem("pow_ready"), sem("r_ready")
        angle_step, angle_ready, trig_ready, nsin_ready = sem("angle_step"), sem("angle_ready"), sem("trig_ready"), sem("nsin_ready")
        k_raw, rope_step, rope_done = sem("k_raw"), sem("rope_step"), sem("rope_done")
        f_step, f_exp, f_one, f_ln, log_f_ready = sem("f_step"), sem("f_exp"), sem("f_one"), sem("f_ln"), sem("log_f_ready")
        decay_done, decay_copied, decay_stored = sem("decay_done"), sem("decay_copied"), sem("decay_stored")
        decay_spread, bias_ready = sem("decay_spread"), sem("bias_ready")
        hi_part = sem("hi_part")
        vb_ready = sem("vb_ready")
        z_tanh = sem("z_tanh")
        scores_done, row_max, neg_max, exp_done = sem("scores_done"), sem("row_max"), sem("neg_max"), sem("exp_done")
        den_ready, rec_ready, inv_ready = sem("den_ready"), sem("rec_ready"), sem("inv_ready")
        pv_done, y_ready = sem("pv_done"), sem("y_ready")
        merged_ready = sem("merged_ready")
        sq_ready = sem("sq_ready")
        ms2_step, pow2_ready, xn_ready = sem("ms2_step"), sem("pow2_ready"), sem("xn_ready")
        gate_step, result_ready = sem("gate_step"), sem("result_ready")
        stored = [sem("stored0"), sem("stored1")]

        decay_dram = nc.dram_tensor("decay_dram", (FOX_HEADS, 3 * P), F32, kind="Internal").ap()
        x_v = x.rearrange("b (t p) d -> p (b t) d", p=P)
        out_v = out.rearrange("b (t p) d -> p (b t) d", p=P)
        w_in_v = w_in.rearrange("a (k p) n -> p (a k) n", p=P)
        fox_v = w_o_fox.rearrange("a (k p) n -> p (a k) n", p=P)
        swa_v = w_o_swa.rearrange("a (k p) n -> p (a k) n", p=P)
        out_w = w_out.rearrange("a (k p) n -> p (a k) n", p=P)
        ple_w = w_ple.rearrange("a (k p) n -> p (a k) n", p=P)
        gate_w = w_ple_gate.rearrange("a (k p) n -> p (a k) n", p=P)

        def width(u):
            return KVF if isinstance(u, int) and u < UPC else N

        def loaded(slot, turn_):
            if isinstance(turn_, int) and turn_ < UPC // RING:
                return 32 * (turn_ + 1)
            return turn_ * 16 + 16 + 16 * (UPC // RING)

        def t_bank(i):
            return tp[i % 2]

        def left(eng, g):
            eng.wait_ge(acc_out[g % 2], g // 2 + 1)

        def t_left(eng, i):
            eng.wait_ge(t_out[i % 2], i // 2 + 1)

        block = ctx.enter_context(nc.Block())

        @block.sync
        def _(sp):
            def load(u, slot, view, k, cols):
                count = sp.lower_val(u - RING + 1)
                dma = sp.dma_start(w_st[:, slot, :, :], view[:, k:k + UK, cols])
                dma.wait_op(lo_ready, count, "sem-ge")
                dma.then_inc(w_loaded[slot], 16)

            for t in range(NT):
                sp.dma_start(x_in[:, t, 0:N], x_v[:, t, 0:N]).then_inc(x_loaded[0], 16)
            for u in range(UPC):
                if u >= RING:
                    sp.wait_ge(lo_ready, u - RING + 1)
                s, k = u % RING, UK * u
                sp.dma_start(w_st[:, s, :, 0:2 * KV_WIDTH],
                             w_in_v[:, k:k + UK, C_KB:C_KB + 2 * KV_WIDTH]).then_inc(w_loaded[s], 16)
                sp.dma_start(w_st[:, s, :, 2 * KV_WIDTH:KVF],
                             w_in_v[:, k:k + UK, C_F:C_F + FOX_HEADS]).then_inc(w_loaded[s], 16)
                if u < 3:
                    for t in range(NT):
                        cols = slice((u + 1) * N, (u + 2) * N)
                        sp.dma_start(x_in[:, t, cols], x_v[:, t, cols]).then_inc(x_loaded[u + 1], 16)
            for c in range(1, NCH):
                for j in range(UPC):
                    load(c * UPC + j, j % RING, w_in_v, UK * j, slice(CHUNKS[c][2], CHUNKS[c][2] + N))
            with sp.Fori(0, NC) as i:
                u = i * MIX_UNITS + U_MIX
                for j in range(UPC):
                    load(u + j, j % RING, w_in_v, UK * j, bass.ds(i * N + C_GA, N))
                for j in range(UPC):
                    load(u + (UPC + j), j % RING, w_in_v, UK * j, bass.ds(i * N + C_GB, N))
                for j in range(UPO):
                    load(u + (2 * UPC + j), j % RING, swa_v, UK * j, bass.ds(i * N, N))
                for j in range(UPO):
                    load(u + (2 * UPC + UPO + j), j % RING, fox_v, UK * j, bass.ds(i * N, N))
            for n in range(E0):
                load(U_E0 + n, (U_E0 + n) % RING, ple_w, 0, slice(n * N, (n + 1) * N))
            with sp.Fori(0, NC) as i:
                u = i * UPC + U_OUT
                for j in range(UPC):
                    load(u + j, (U_OUT + j) % RING, out_w, UK * j, bass.ds(i * N, N))
                    if j == UPC - 2:
                        sp.dma_start(x_res[:, :, bass.ds(i * N, N)], x_v[:, :, bass.ds(i * N, N)]).then_inc(late_loaded[0], 16)
                        sp.dma_start(g2_sb[:, bass.ds(i * N, N)],
                                     post_norm_g[0, bass.ds(i * N, N)].partition_broadcast(P)).then_inc(late_loaded[1], 16)
            for n in range(E1):
                load(U_E1 + n, (U_E1 + n) % RING, ple_w, 0, slice((E0 + n) * N, (E0 + n + 1) * N))
            with sp.Fori(0, NC) as i:
                u = i * UPC + U_GATE
                for j in range(UPC):
                    load(u + j, j % RING, gate_w, UK * j, bass.ds(i * N, N))
            sp.wait_ge(result_ready, NC)
            sp.dma_start(out_v[:, :, (NC - 1) * N:], sg[:, (NC - 1) % 2, :, :]).then_inc(stored[(NC - 1) % 2], 16)
            for s in stored:
                sp.wait_ge(s, 16 * NC // 2)

        @block.gpsimd
        def _(pool):
            pool.memset(ident[:, :], 0.0).then_inc(const_ready, 1)
            pool.wait_ge(const_ready, 1)
            pool.affine_select(out=ident[:, :], in_=ident[:, :], compare_op=ALU.not_equal, fill=1.0,
                               base=0, pattern=[[-1, P]], channel_multiplier=1).then_inc(ident_ready, 1)
            pool.memset(rms[:, 1, :], -0.5)
            pool.memset(rms2[:, 1, :], -0.5)
            pool.memset(mask[:, :, :], 0.0)
            pool.memset(tri[:, :], -1.0).then_inc(const_ready, 1)
            pool.wait_ge(const_ready, 2)
            for m in range(2):
                for b in (0, 2):
                    v = mask[:, m, b * P:(b + 1) * P]
                    pool.affine_select(out=v, in_=v, compare_op=ALU.is_ge, fill=MASKED, base=0,
                                       pattern=[[-1, P]], channel_multiplier=1).then_inc(masks_ready, 1)
            v = mask[:, 1, P:2 * P]
            pool.affine_select(out=v, in_=v, compare_op=ALU.is_gt, fill=MASKED, base=0,
                               pattern=[[1, P]], channel_multiplier=-1).then_inc(masks_ready, 1)
            for b in range(2):
                v = tri[:, b * P:(b + 1) * P]
                pool.affine_select(out=v, in_=v, compare_op=ALU.is_ge, fill=0.0, base=0,
                                   pattern=[[1, P]], channel_multiplier=-1).then_inc(masks_ready, 1)
            pool.wait_ge(ms_ready, 1)
            pool.tensor_tensor(rms[:, 2, :], rms[:, 0, :], rms[:, 1, :], ALU.pow).then_inc(pow_ready, 1)
            pool.wait_ge(nsin_ready, 1)
            steps = 0
            for c in range(3):
                heads = SWA_KV if c == 0 else N // SWA_DIM
                w = heads * SWA_DIM
                if c == 0:
                    pool.wait_ge(k_raw, 1)
                else:
                    left(pool, c)
                if c:
                    pool.wait_ge(t_done, T_INDEX[("kbT", 0) if c == 1 else ("qbT", 1)] + 1)
                src = raw[:, :, 0:w].rearrange("p t (h a d) -> p t h a d", a=2, d=HALF)
                tmp = rtmp[:, :, 0:w].rearrange("p t (h a d) -> p t h a d", a=2, d=HALF)
                for t in range(NT):
                    pool.tensor_tensor(rtmp[:, t, 0:w].rearrange("p (h d) -> p h d", d=HALF),
                                       raw[:, t, 0:w].rearrange("p (h d) -> p h d", d=HALF),
                                       trig[:, 1:2, t, :].to_broadcast([P, 2 * heads, HALF]), ALU.mult)
                for t in range(NT):
                    for a in range(2):
                        r_ = pool.tensor_tensor(
                            rot[:, t, 0:w].rearrange("p (h a d) -> p h a d", a=2, d=HALF)[:, :, a, :]
                            if c else rot[:, t, 2 * w:3 * w].rearrange("p (h a d) -> p h a d", a=2, d=HALF)[:, :, a, :],
                            src[:, t, :, 1 - a, :],
                            trig[:, 2 * (1 - a):2 * (1 - a) + 1, t, :].to_broadcast([P, heads, HALF]), ALU.mult)
                r_.then_inc(rope_step, 1)
                steps += 1
                pool.wait_ge(rope_step, steps)
                if c:
                    pool.tensor_tensor(rot[:, :, :], rtmp[:, :, :], rot[:, :, :], ALU.add).then_inc(rope_done, 1)
                else:
                    for kv in range(SWA_KV):
                        for dup in range(2):
                            r_ = pool.tensor_tensor(
                                rot[:, :, (2 * kv + dup) * SWA_DIM:(2 * kv + dup + 1) * SWA_DIM],
                                rtmp[:, :, kv * SWA_DIM:(kv + 1) * SWA_DIM],
                                rot[:, :, 2 * w + kv * SWA_DIM:2 * w + (kv + 1) * SWA_DIM], ALU.add)
                    r_.then_inc(rope_done, 1)
            pool.wait_ge(ms2_step, 2)
            pool.tensor_tensor(rms2[:, 2, :], rms2[:, 0, :], rms2[:, 1, :], ALU.pow).then_inc(pow2_ready, 1)

        @block.scalar
        def _(act):
            act.dma_start(pos_i[:, :], positions).then_inc(pos_loaded, 16)
            act.dma_start(inv_sb[:, :], inv_freq.partition_broadcast(P)).then_inc(pos_loaded, 16)
            act.dma_start(g1T[:, :], pre_norm_g).then_inc(g1_loaded, 16)
            act.dma_start(bf_sb[:, :], b_forget[0].partition_broadcast(P)).then_inc(small_loaded, 16)
            act.dma_start(sink_sb[:, :], sinks[0].partition_broadcast(P)).then_inc(small_loaded, 16)
            act.dma_start(p_in[:, :, :], p.rearrange("a b (t p) d -> p (a b t) d", p=P)).then_inc(p_loaded, 16)
            act.wait_ge(angle_ready, 1)
            act.activation(trig[:, 0:2, :, :], ang[:, :, :, :], ACT.Sin).then_inc(trig_ready, 1)

            def w_high(u, slot, turn_):
                act.wait_ge(w_loaded[slot], loaded(slot, turn_))
                if not isinstance(u, int) or u >= RING:
                    act.wait_ge(unit_done, u - RING + 1)
                w = width(u)
                act.activation(w_hi[:, slot, :, 0:w], w_st[:, slot, :, 0:w], ACT.Copy).then_inc(hi_ready, 1)

            def x_high(j):
                act.wait_ge(xT_done, j + 1)
                for k in range(2):
                    r_ = act.activation(hT_hi[:, 2 * j + k, :], four[j % 4][:, k * SEQ:(k + 1) * SEQ], ACT.Copy,
                                        scale=g1T[:, 2 * j + k:2 * j + k + 1])
                r_.then_inc(hT_hi_ready, 1)

            def evacuate(c):
                what, g, _ = CHUNKS[c]
                a = acc[c % 2]
                act.wait_ge(unit_done, UPC * (c + 1))
                if what == "kvf":
                    act.wait_ge(r_ready, 1)
                    for dst, cols, ready in ((raw[:, :, 0:KV_WIDTH], slice(0, KV_WIDTH), k_raw),
                                             (vb, slice(KV_WIDTH, 2 * KV_WIDTH), vb_ready),
                                             (fg[:, 0, :, :], slice(2 * KV_WIDTH, KVF), acc_out[0])):
                        for t in range(NT):
                            r_ = act.activation(dst[:, t, :], a[:, t, cols], ACT.Copy, scale=rms[:, 2, t:t + 1])
                        r_.then_inc(ready, 1)
                elif what in ("qb", "qa", "ka"):
                    if what == "qb" and g == 0:
                        act.wait_ge(rope_done, 1)
                    if what == "qb" and g == 1:
                        act.wait_ge(rope_done, 2)
                    if what == "qa" and g == 0:
                        act.wait_ge(rope_done, 3)
                    which = 4 if what == "qa" else 2
                    for t in range(NT):
                        r_ = act.activation(raw[:, t, :], a[:, t, :], ACT.Copy, scale=rms[:, which, t:t + 1])
                    r_.then_inc(acc_out[c % 2], 1)
                elif what == "va":
                    for t in range(NT):
                        r_ = act.activation(va[:, t, g * N:(g + 1) * N], a[:, t, :], ACT.Copy, scale=rms[:, 2, t:t + 1])
                    r_.then_inc(acc_out[c % 2], 1)
                else:
                    dst = szb if what == "zb" else sza
                    act.wait_ge(sumsq_ready, 2)
                    for t in range(NT):
                        r_ = act.activation(dst[:, t, g * N:(g + 1) * N], a[:, t, :], ACT.Tanh, scale=rms[:, 3, t:t + 1])
                    r_.then_inc(z_tanh, 1)

            def exps(h):
                act.wait_ge(neg_max, h + 1)
                b = probs[:, h % 2, :]
                for t, cols in ((0, slice(0, P)), (1, slice(P, 3 * P))):
                    r_ = act.activation(b[:, cols], b[:, cols], ACT.Exp, bias=row[:, 1, h, t:t + 1],
                                        accum_out=row[:, 2, h, t:t + 1])
                if h < SWA_HEADS:
                    r_ = act.activation(row[:, 3, h, :], row[:, 1, h, :], ACT.Exp, bias=sink_sb[:, h:h + 1])
                r_.then_inc(exp_done, 1)

            def copy_out(what, n):
                i = T_INDEX[(what, n)]
                act.wait_ge(t_done, i + 1)
                src = t_bank(i)
                if what == "probs":
                    if n >= 2:
                        act.wait_ge(pv_done, n - 1)
                    act.activation(probsT[:, n % 2, :], src[:, 0:3 * P], ACT.Copy).then_inc(t_out[i % 2], 1)
                elif what in ("y", "pT"):
                    w = 2 * SEQ if what == "pT" else SEQ
                    dst = pT_hi[:, :, :] if what == "pT" else yT_hi[:, n:n + 1, :]
                    act.activation(dst, src[:, 0:w].rearrange("p (k s) -> p k s", s=SEQ), ACT.Copy).then_inc(hi_part, 1)
                else:
                    dst = {"kbT": kbT, "qbT": qbT, "qaT": qaT, "kaT": kaT}[what]
                    scale = SWA_DIM ** -0.5 if what == "qbT" else 1.0
                    act.activation(dst[:, 2 * n:2 * n + 2, :], src[:, :].rearrange("p (k s) -> p k s", s=SEQ),
                                   ACT.Copy, scale=scale).then_inc(t_out[i % 2], 1)

            def after(u):
                if u < 4:
                    x_high(u + 4)
                if u in (1, 2):
                    t = u - 1
                    act.activation((sza, szb)[t][:, :, :], x_in[:, t, :].rearrange("p (a n) -> p a n", a=NT), ACT.Square,
                                   accum_out=sumsq[:, t:t + 1]).then_inc(sumsq_ready, 1)
                if u % UPC == UPC - 1 and u < U_MIX:
                    evacuate(u // UPC)
                if u == 8:
                    act.wait_ge(f_step, 3)
                    act.activation(fg[:, 2, :, :], fg[:, 1, :, :], ACT.Exp, scale=-1.0).then_inc(f_exp, 1)
                if u == 9:
                    act.wait_ge(f_one, 1)
                    act.activation(fg[:, 3, :, :], fg[:, 2, :, :], ACT.Ln).then_inc(f_ln, 1)
                if u == DECAY_AT:
                    act.wait_ge(decay_done, 1)
                    act.activation(decay_rows, sc[0:FOX_HEADS, 0:3 * P], ACT.Copy).then_inc(decay_copied, 1)
                if u == DECAY_AT + 1:
                    act.wait_ge(decay_copied, 1)
                    act.dma_start(decay_dram[:, :], decay_rows).then_inc(decay_stored, 16)
                if u == DECAY_AT + 3:
                    act.wait_ge(decay_stored, 16)
                    act.dma_start(bias[:, :, :], decay_dram.partition_broadcast(P)).then_inc(decay_spread, 16)
                if u - 1 in HEAD_AT:
                    exps(HEAD_AT[u - 1])
                for use in T_AT.get(u, ()):
                    copy_out(*use)

            def gate_tanh(slot_g):
                for t in range(NT):
                    r_ = act.activation(sg[:, slot_g, t, :], acc[(G_MIX + slot_g) % 2][:, t, :], ACT.Tanh,
                                        scale=rms[:, 3, t:t + 1])
                r_.then_inc(acc_out[(G_MIX + slot_g) % 2], 1)

            def merged_high(i, s):
                n = T_MIX + s
                act.wait_ge(t_done, i * 2 + (n + 1))
                act.activation(mT_hi[:, bass.ds(i * 4 + 2 * s, 2), :] if not isinstance(i, int) else mT_hi[:, 4 * i + 2 * s:4 * i + 2 * s + 2, :],
                               t_bank(n)[:, :].rearrange("p (k s) -> p k s", s=SEQ), ACT.Copy, scale=0.5).then_inc(hi_part, 1)

            def mix(i):
                u = i * MIX_UNITS + U_MIX
                turn_ = i * (MIX_UNITS // RING) + (U_MIX // RING)
                for j in range(MIX_UNITS):
                    w_high(u + (j + RING), j % RING, turn_ + (j // RING + 1))
                    if isinstance(i, int):
                        after(u + j)
                    if not isinstance(i, int) and j == 1:
                        for s in range(2):
                            merged_high(i - 1, s)
                    if j in (UPC - 1, 2 * UPC - 1):
                        which = j // UPC
                        act.wait_ge(unit_done, u + (j + 1))
                        gate_tanh(which)

            for u in range(RING):
                if u == 0:
                    act.wait_ge(g1_loaded, 16)
                x_high(u)
                w_high(u, u, 0)
            for u in range(U_MIX):
                w_high(u + RING, u % RING, u // RING + 1)
                after(u)
            mix(0)
            with act.Fori(1, NC) as i:
                mix(i)

            def last_tanh(n):
                g = G_GATE + n
                act.wait_ge(unit_done, U_GATE + UPC * (n + 1))
                if n >= 2:
                    act.wait_ge(stored[n % 2], 16 * (n // 2))
                act.activation(sg[:, n % 2, :, :], acc[g % 2][:, :, :], ACT.Tanh, scale=0.5).then_inc(acc_out[g % 2], 1)

            for u in range(U_E0, U_END):
                if u + RING < U_END:
                    w_high(u + RING, u % RING, u // RING + 1)
                if u < U_OUT or U_E1 <= u < U_GATE:
                    n = u - U_E0 if u < U_OUT else E0 + u - U_E1
                    g = G_E0 + n if n < E0 else G_E1 + n - E0
                    act.wait_ge(unit_done, u + 1)
                    act.activation(ple[:, :, n * N:(n + 1) * N], acc[g % 2][:, :, :], ACT.Copy, scale=0.5).then_inc(acc_out[g % 2], 1)
                if u == U_OUT - 1:
                    for s in range(2):
                        merged_high(NC - 1, s)
                if U_OUT <= u < U_E1 and (u - U_OUT) % UPC == UPC - 1:
                    n = (u - U_OUT) // UPC
                    act.wait_ge(unit_done, u + 1)
                    for t in range(NT):
                        r_ = act.activation(sg[:, 0, t, :], acc[(G_OUT + n) % 2][:, t, :], ACT.Square,
                                            accum_out=sumsq2[:, n, t:t + 1])
                    r_.then_inc(sq_ready, 1)
                for j in XN_AT.get(u, ()):
                    i = T_XN + j
                    act.wait_ge(t_done, i + 1)
                    act.activation(hT_hi[:, 2 * j:2 * j + 2, :], t_bank(i)[:, :].rearrange("p (k s) -> p k s", s=SEQ),
                                   ACT.Copy).then_inc(hi_part, 1)
                if u >= U_GATE and (u - U_GATE) % UPC == UPC - 1:
                    last_tanh((u - U_GATE) // UPC)
                if u >= U_GATE + UPC and (u - U_GATE) % UPC == 1:
                    n = (u - U_GATE) // UPC - 1
                    act.wait_ge(result_ready, n + 1)
                    act.dma_start(out_v[:, :, n * N:(n + 1) * N], sg[:, n % 2, :, :]).then_inc(stored[n % 2], 16)

        @block.vector
        def _(dve):
            dve.wait_ge(pos_loaded, 32)
            dve.tensor_copy(pos_f[:, :], pos_i[:, :]).then_inc(angle_step, 1)
            dve.wait_ge(angle_step, 1)
            for t in range(NT):
                for a in range(2):
                    r_ = dve.tensor_scalar(ang[:, a, t, :], inv_sb[:, :], pos_f[:, t:t + 1], None, ALU.mult)
            r_.then_inc(angle_step, 1)
            dve.wait_ge(angle_step, 2)
            for a in range(2):
                r_ = dve.tensor_scalar(turn[:, a, :, :], ang[:, a, :, :], 1.0 / (2.0 * np.pi), 0.25 * a,
                                       ALU.mult, ALU.add)
            r_.then_inc(angle_step, 1)
            dve.wait_ge(angle_step, 3)
            dve.tensor_scalar(turn[:, :, :, :], turn[:, :, :, :], ROUND, -ROUND, ALU.add, ALU.add).then_inc(angle_step, 1)
            for n, part in enumerate((TWO_PI_1, TWO_PI_2, TWO_PI_3)):
                dve.wait_ge(angle_step, 4 + n)
                dve.scalar_tensor_tensor(out=ang[:, :, :, :], in0=turn[:, :, :, :], scalar=-part, in1=ang[:, :, :, :],
                                         op0=ALU.mult, op1=ALU.add).then_inc(angle_step, 1)
            dve.wait_ge(angle_step, 7)
            dve.tensor_scalar(ang[:, 1, :, :], ang[:, 1, :, :], 0.5 * np.pi, None, ALU.add).then_inc(angle_step, 1)
            dve.wait_ge(angle_step, 8)
            dve.tensor_scalar(ang[:, :, :, :], ang[:, :, :, :], PI_BELOW, -PI_BELOW, ALU.min, ALU.max).then_inc(angle_ready, 1)
            dve.wait_ge(trig_ready, 1)
            dve.tensor_scalar(trig[:, 2, :, :], trig[:, 0, :, :], -1.0, None, ALU.mult).then_inc(nsin_ready, 1)

            def w_low(u, slot):
                dve.wait_ge(hi_ready, u + 1)
                w = width(u)
                dve.tensor_tensor(w_lo[:, slot, :, 0:w], w_st[:, slot, :, 0:w], w_hi[:, slot, :, 0:w].bitcast(F32),
                                  ALU.subtract).then_inc(lo_ready, 1)

            def x_low(j):
                dve.wait_ge(hT_hi_ready, j + 1)
                for k in range(2):
                    kk = 2 * j + k
                    r_ = dve.scalar_tensor_tensor(out=hT_lo[:, kk, :], in0=four[j % 4][:, k * SEQ:(k + 1) * SEQ],
                                                  scalar=g1T[:, kk:kk + 1], in1=hT_hi[:, kk, :].bitcast(F32),
                                                  op0=ALU.mult, op1=ALU.subtract)
                r_.then_inc(hT_ready, 1)

            def split_low(dst_lo, dst_hi, n_hi, i, scale=1.0):
                dve.wait_ge(hi_part, n_hi)
                w = dst_hi.shape[1] * SEQ
                dve.scalar_tensor_tensor(out=dst_lo, in0=t_bank(i)[:, 0:w].rearrange("p (k s) -> p k s", s=SEQ), scalar=scale,
                                         in1=dst_hi.bitcast(F32), op0=ALU.mult, op1=ALU.subtract).then_inc(t_out[i % 2], 1)

            def silu(c):
                what, g, _ = CHUNKS[c]
                n = [i for i, x_ in enumerate(CHUNKS) if x_[0] in ("zb", "za")].index(c)
                v = (szb if what == "zb" else sza)[:, :, g * N:(g + 1) * N]
                dve.wait_ge(z_tanh, n + 1)
                dve.scalar_tensor_tensor(out=v, in0=v, scalar=1.0, in1=acc[c % 2][:, :, :], op0=ALU.add,
                                         op1=ALU.mult).then_inc(acc_out[c % 2], 1)

            def softmax_max(h):
                dve.wait_ge(scores_done, h + 1)
                if h >= 2:
                    dve.wait_ge(t_done, T_INDEX[("probs", h - 2)] + 1)
                b = mask[:, 1, :] if h < SWA_HEADS else bias[:, h - SWA_HEADS, :]
                for t, cols in ((0, slice(0, P)), (1, slice(P, 3 * P))):
                    r_ = dve.tensor_tensor_reduce(probs[:, h % 2, cols], sc[:, cols], b[:, cols], 1.0, -3e38, ALU.add,
                                                  ALU.max, row[:, 0, h, t:t + 1])
                r_.then_inc(row_max, 1)
                dve.wait_ge(row_max, h + 1)
                if h < SWA_HEADS:
                    dve.tensor_scalar(row[:, 1, h, :], row[:, 0, h, :], sink_sb[:, h:h + 1], -1.0, ALU.max,
                                      ALU.mult).then_inc(neg_max, 1)
                else:
                    dve.tensor_scalar(row[:, 1, h, :], row[:, 0, h, :], -1.0, None, ALU.mult).then_inc(neg_max, 1)

            def denominators(h):
                dve.wait_ge(exp_done, h + 1)
                which = 2
                if h < SWA_HEADS:
                    dve.tensor_tensor(row[:, 4, h, :], row[:, 2, h, :], row[:, 3, h, :], ALU.add).then_inc(den_ready, 1)
                    dve.wait_ge(den_ready, h + 1)
                    which = 4
                dve.reciprocal(row[:, 5, h, :], row[:, which, h, :]).then_inc(rec_ready, 1)
                dve.wait_ge(rec_ready, h + 1)
                dve.tensor_tensor(row[:, 5, h, :], row[:, 5, h, :], rms[:, 3, :], ALU.mult).then_inc(inv_ready, 1)

            def gated_values(h):
                fox = h >= SWA_HEADS
                q = SWA_HEADS // 2 + h - SWA_HEADS if fox else h // 2
                d = FOX_DIM if fox else SWA_DIM
                off = 0 if fox else (h % 2) * SWA_DIM
                zcol = ((h - SWA_HEADS) if fox else h) * d
                dve.wait_ge(pv_done, h + 1)
                dve.wait_ge(inv_ready, h + 1)
                left(dve, [c for c, x_ in enumerate(CHUNKS) if x_[0] == ("za" if fox else "zb")][zcol // N])
                if q >= 2 and off == 0:
                    dve.wait_ge(t_done, T_INDEX[("y", q - 2)] + 1)
                z = sza if fox else szb
                for t in range(NT):
                    r_ = dve.scalar_tensor_tensor(out=ybuf[:, q % 2, t, off:off + d], in0=ov[:, t * d:(t + 1) * d],
                                                  scalar=row[:, 5, h, t:t + 1], in1=z[:, t, zcol:zcol + d],
                                                  op0=ALU.mult, op1=ALU.mult)
                r_.then_inc(y_ready, 1)

            splits = [use[1:] for use in T_USES if use[1] in ("y", "pT")]

            def after(u):
                if u < 4:
                    x_low(u + 4)
                if u == 3:
                    dve.wait_ge(sumsq_ready, 2)
                    dve.tensor_scalar(rms[:, 0, :], sumsq[:, :], 1.0 / D_MODEL, EPS, ALU.mult, ALU.add).then_inc(ms_ready, 1)
                if u == 5:
                    dve.wait_ge(pow_ready, 1)
                    dve.tensor_scalar(rms[:, 3, :], rms[:, 2, :], 0.5, None, ALU.mult)
                    dve.tensor_scalar(rms[:, 4, :], rms[:, 2, :], FOX_DIM ** -0.5, None, ALU.mult).then_inc(r_ready, 1)
                if u == UPC - 1:
                    left(dve, 0)
                    dve.wait_ge(small_loaded, 32)
                    for t in range(NT):
                        r_ = dve.tensor_tensor(fg[:, 0, t, :], fg[:, 0, t, :], bf_sb[:, :], ALU.add)
                    r_.then_inc(f_step, 1)
                    dve.wait_ge(f_step, 1)
                    dve.tensor_scalar(fg[:, 1, :, :], fg[:, 0, :, :], -1.0, None, ALU.mult).then_inc(f_step, 1)
                    dve.wait_ge(f_step, 2)
                    dve.tensor_tensor(fg[:, 1, :, :], fg[:, 0, :, :], fg[:, 1, :, :], ALU.max).then_inc(f_step, 1)
                    dve.tensor_scalar(log_f[:, :, :], fg[:, 0, :, :], 0.0, None, ALU.min).then_inc(f_step, 1)
                if u == 8:
                    dve.wait_ge(f_exp, 1)
                    dve.tensor_scalar(fg[:, 2, :, :], fg[:, 2, :, :], 1.0, None, ALU.add).then_inc(f_one, 1)
                if u == 10:
                    dve.wait_ge(f_ln, 1)
                    dve.wait_ge(f_step, 4)
                    dve.tensor_tensor(log_f[:, :, :], log_f[:, :, :], fg[:, 3, :, :], ALU.subtract).then_inc(log_f_ready, 1)
                if u == BIAS_AT:
                    dve.wait_ge(decay_spread, 16)
                    dve.wait_ge(masks_ready, 7)
                    dve.tensor_tensor(bias[:, :, :], bias[:, :, :], mask[:, 0:1, :].to_broadcast([P, FOX_HEADS, 3 * P]),
                                      ALU.add).then_inc(bias_ready, 1)
                if u in HEAD_AT:
                    softmax_max(HEAD_AT[u])
                if u - 2 in HEAD_AT:
                    denominators(HEAD_AT[u - 2])
                if u - 3 in HEAD_AT:
                    gated_values(HEAD_AT[u - 3])
                for what, n in T_AT.get(u, ()):
                    if what in ("y", "pT"):
                        i = T_INDEX[(what, n)]
                        hi, lo = (pT_hi[:, :, :], pT_lo[:, :, :]) if what == "pT" else (yT_hi[:, n:n + 1, :], yT_lo[:, n:n + 1, :])
                        split_low(lo, hi, splits.index((what, n)) + 1, i)
                if u % UPC == UPC - 1 and u < U_MIX and CHUNKS[u // UPC][0] in ("zb", "za"):
                    silu(u // UPC)

            def merged_low(i, s):
                n = T_MIX + s
                if isinstance(i, int):
                    lo, hi = (m[:, 4 * i + 2 * s:4 * i + 2 * s + 2, :] for m in (mT_lo, mT_hi))
                else:
                    lo, hi = (m[:, bass.ds(i * 4 + 2 * s, 2), :] for m in (mT_lo, mT_hi))
                split_low(lo, hi, i * 2 + (len(splits) + s + 1), n, 0.5)

            def mix(i):
                u = i * MIX_UNITS + U_MIX
                for j in range(MIX_UNITS):
                    w_low(u + (j + RING), j % RING)
                    if isinstance(i, int):
                        after(u + j)
                    if not isinstance(i, int) and j == 1:
                        for s in range(2):
                            merged_low(i - 1, s)
                    for g, last in ((1, 2 * UPC + UPO - 1), (0, MIX_UNITS - 1)):
                        if j == last:
                            n = (G_MIX + g) // 2 + 1
                            dve.wait_ge(unit_done, u + (j + 1))
                            dve.wait_ge(acc_out[(G_MIX + g) % 2], i * 2 + n)
                            bank = (G_MIX + 3 - g) % 2
                            dve.scalar_tensor_tensor(out=sg[:, g, :, :], in0=sg[:, g, :, :], scalar=1.0, in1=acc[bank][:, :, :],
                                                     op0=ALU.add, op1=ALU.mult).then_inc(acc_out[bank], 1)
                    if j == MIX_UNITS - 1:
                        for g in (2, 3):
                            dve.wait_ge(acc_out[(G_MIX + g) % 2], i * 2 + ((G_MIX + g) // 2 + 1))
                        dve.tensor_tensor(sg[:, 0, :, :], sg[:, 0, :, :], sg[:, 1, :, :], ALU.add).then_inc(merged_ready, 1)

            for u in range(RING):
                x_low(u)
                w_low(u, u)
            for u in range(U_MIX):
                w_low(u + RING, u % RING)
                after(u)
            mix(0)
            with dve.Fori(1, NC) as i:
                mix(i)

            def x_piece(j):
                cols = slice(2 * P * j, 2 * P * (j + 1))
                for t in range(NT):
                    r_ = dve.scalar_tensor_tensor(out=x_new[:, t, cols], in0=x_new[:, t, cols], scalar=rms2[:, 2, t:t + 1],
                                                  in1=x_res[:, t, cols], op0=ALU.mult, op1=ALU.add)
                r_.then_inc(xn_ready, 1)

            for u in range(U_E0, U_END):
                if u + RING < U_END:
                    w_low(u + RING, u % RING)
                if u == U_OUT - 1:
                    for s in range(2):
                        merged_low(NC - 1, s)
                if U_OUT <= u < U_E1 and (u - U_OUT) % UPC == UPC - 1:
                    n = (u - U_OUT) // UPC
                    g = G_OUT + n
                    dve.wait_ge(late_loaded[1], 16 * (n + 1))
                    dve.wait_ge(sq_ready, n + 1)
                    for t in range(NT):
                        r_ = dve.tensor_tensor(x_new[:, t, n * N:(n + 1) * N], acc[g % 2][:, t, :], g2_sb[:, n * N:(n + 1) * N],
                                               ALU.mult)
                    r_.then_inc(acc_out[g % 2], 1)
                if u == U_E1 - 1:
                    dve.tensor_reduce(rms2[:, 0, :], sumsq2[:, :, :].rearrange("p n t -> p t n"), AX.X, ALU.add).then_inc(ms2_step, 1)
                    dve.wait_ge(ms2_step, 1)
                    dve.tensor_scalar(rms2[:, 0, :], rms2[:, 0, :], 1.0 / D_MODEL, EPS, ALU.mult, ALU.add).then_inc(ms2_step, 1)
                    dve.wait_ge(pow2_ready, 1)
                    dve.wait_ge(late_loaded[0], 16 * NC)
                    left(dve, G_OUT + NC - 2)
                    left(dve, G_OUT + NC - 1)
                    x_piece(0)
                    x_piece(1)
                for j in XN_AT.get(u, ()):
                    i = T_XN + j
                    split_low(hT_lo[:, 2 * j:2 * j + 2, :], hT_hi[:, 2 * j:2 * j + 2, :],
                              len(splits) + 2 * NC + j + 1, i)
                if U_GATE - 2 <= u < U_GATE + UPC - 4:
                    x_piece(u - U_GATE + 4)
                if u >= U_GATE and (u - U_GATE) % UPC == UPC - 1:
                    n = (u - U_GATE) // UPC
                    cols = slice(n * N, (n + 1) * N)
                    v = sg[:, n % 2, :, :]
                    left(dve, G_GATE + n)
                    left(dve, G_GATE - 2)
                    left(dve, G_GATE - 1)
                    dve.scalar_tensor_tensor(out=v, in0=v, scalar=1.0, in1=ple[:, :, cols], op0=ALU.add,
                                             op1=ALU.mult).then_inc(gate_step, 1)
                    dve.wait_ge(gate_step, n + 1)
                    dve.tensor_tensor(v, v, x_new[:, :, cols], ALU.add).then_inc(result_ready, 1)

        @block.tensor
        def _(pe):
            def x_transposes(j):
                if j >= 4:
                    pe.wait_ge(hT_ready, j - 3)
                pe.wait_ge(x_loaded[j // 2], 32)
                for k in range(2):
                    for t in range(NT):
                        r_ = pe.transpose(four[j % 4][:, (2 * k + t) * P:(2 * k + t + 1) * P],
                                          x_in[:, t, (2 * j + k) * P:(2 * j + k + 1) * P], ident[:, :])
                r_.then_inc(xT_done, 1)

            def unit(u, slot, bank, lhs_hi, lhs_lo, k0, first, last, w=N):
                pe.wait_ge(lo_ready, u + 1)
                for k in range(UK):
                    for t in range(NT):
                        hi = lhs_hi[:, k0 + k, t * P:(t + 1) * P]
                        lo = lhs_lo[:, k0 + k, t * P:(t + 1) * P]
                        o = bank[:, t, 0:w]
                        pe.matmul(o, hi, w_hi[:, slot, k, 0:w], start=(first and k == 0), stop=False)
                        pe.matmul(o, hi, w_lo[:, slot, k, 0:w], start=False, stop=False)
                        r_ = pe.matmul(o, lo, w_hi[:, slot, k, 0:w], start=False, stop=(last and k == UK - 1))
                r_.then_inc(unit_done, 1)

            def transposes(what, n):
                i = T_INDEX[(what, n)]
                bank = t_bank(i)
                if i >= 2:
                    pe.wait_ge(t_out[i % 2], i // 2)
                if what == "probs":
                    pe.wait_ge(exp_done, n + 1)
                    src = [probs[:, n % 2, b * P:(b + 1) * P] for b in range(3)]
                elif what == "y":
                    pe.wait_ge(y_ready, 2 * n + 2 if n < SWA_HEADS // 2 else SWA_HEADS + n - SWA_HEADS // 2 + 1)
                    src = [ybuf[:, n % 2, t, :] for t in range(NT)]
                elif what == "pT":
                    pe.wait_ge(p_loaded, 16)
                    src = [p_in[:, t, k * P:(k + 1) * P] for k in range(2) for t in range(NT)]
                elif what in ("kbT", "qbT"):
                    pe.wait_ge(rope_done, 1 if what == "kbT" else 2 + n // 2)
                    src = [rot[:, t, (2 * (n % 2) + k) * P:(2 * (n % 2) + k + 1) * P] for k in range(2) for t in range(NT)]
                else:
                    left(pe, CHUNKS.index((what[0:2], n // 2, (C_QA if what == "qaT" else C_KA) + n // 2 * N)))
                    src = [raw[:, t, (2 * (n % 2) + k) * P:(2 * (n % 2) + k + 1) * P] for k in range(2) for t in range(NT)]
                for b, s in enumerate(src):
                    r_ = pe.transpose(bank[:, b * P:(b + 1) * P], s, ident[:, :])
                r_.then_inc(t_done, 1)

            def decay():
                pe.wait_ge(log_f_ready, 1)
                pe.wait_ge(masks_ready, 7)
                pe.matmul(sc[0:FOX_HEADS, 0:3 * P], log_f[:, 0, :], tri[:, :], start=True, stop=False)
                pe.matmul(sc[0:FOX_HEADS, 2 * P:3 * P], log_f[:, 1, :], tri[:, 0:P], start=False,
                          stop=True).then_inc(decay_done, 1)

            def scores(h):
                if h == 0:
                    pe.wait_ge(decay_copied, 1)
                    t_left(pe, T_INDEX[("qbT", 3)])
                    t_left(pe, T_INDEX[("qbT", 2)])
                    t_left(pe, T_INDEX[("kbT", 0)])
                else:
                    pe.wait_ge(row_max, h)
                if h < SWA_HEADS:
                    rows = slice((h % 2) * SWA_DIM, (h % 2 + 1) * SWA_DIM)
                    q, k = qbT[rows, h // 2, :], kbT[rows, h // GROUP, :]
                else:
                    f = h - SWA_HEADS
                    if f % 4 == 0:
                        for n in range(2):
                            t_left(pe, T_INDEX[("qaT", 2 * (f // 4) + n)])
                            t_left(pe, T_INDEX[("kaT", 2 * (f // 4) + n)])
                    q, k = qaT[:, f, :], kaT[:, f, :]
                pe.matmul(sc[:, 0:P], q[:, 0:P], k[:, 0:P], start=True, stop=True)
                pe.matmul(sc[:, P:3 * P], q[:, P:SEQ], k, start=True, stop=True).then_inc(scores_done, 1)

            def values(h):
                d = SWA_DIM if h < SWA_HEADS else FOX_DIM
                v, c = (vb, h // GROUP * d) if h < SWA_HEADS else (va, (h - SWA_HEADS) * d)
                t_left(pe, T_INDEX[("probs", h)])
                if h < SWA_HEADS:
                    pe.wait_ge(vb_ready, 1)
                else:
                    left(pe, [c_ for c_, x_ in enumerate(CHUNKS) if x_[0] == "va"][(h - SWA_HEADS) // 4])
                if h >= 1:
                    pe.wait_ge(y_ready, h)
                pT = probsT[:, h % 2, :]
                pe.matmul(ov[:, 0:d], pT[:, 0:P], v[:, 0, c:c + d], start=True, stop=True)
                pe.matmul(ov[:, d:2 * d], pT[:, P:2 * P], v[:, 0, c:c + d], start=True, stop=False)
                pe.matmul(ov[:, d:2 * d], pT[:, 2 * P:3 * P], v[:, 1, c:c + d], start=False, stop=True).then_inc(pv_done, 1)

            def after(u):
                if u < 4:
                    x_transposes(u + 4)
                if u == DECAY_AT:
                    decay()
                if u - 3 in HEAD_AT:
                    values(HEAD_AT[u - 3])
                if u in HEAD_AT:
                    scores(HEAD_AT[u])
                for use in T_AT.get(u, ()):
                    transposes(*use)

            def group_start(g_slot, uses):
                pe.wait_ge(acc_out[g_slot], uses)

            pe.wait_ge(ident_ready, 1)
            for j in range(4):
                x_transposes(j)
            for u in range(U_MIX):
                c, j = u // UPC, u % UPC
                if c == 0:
                    pe.wait_ge(hT_ready, j + 1)
                if j == 0 and c >= 2:
                    group_start(c % 2, c // 2)
                unit(u, u % RING, acc[c % 2], hT_hi, hT_lo, UK * j, j == 0, j == UPC - 1, width(u))
                after(u)

            def merged_transposes(i):
                pe.wait_ge(merged_ready, i + 1)
                for s in range(2):
                    n = T_MIX + s
                    pe.wait_ge(t_out[n % 2], i + n // 2)
                    for k in range(2):
                        for t in range(NT):
                            r_ = pe.transpose(t_bank(n)[:, (2 * k + t) * P:(2 * k + t + 1) * P],
                                              sg[:, 0, t, (2 * s + k) * P:(2 * s + k + 1) * P], ident[:, :])
                    r_.then_inc(t_done, 1)

            def mix(i):
                u = i * MIX_UNITS + U_MIX
                for j in range(MIX_UNITS):
                    if j < 2 * UPC:
                        g, jj, n_units, k_off, hi, lo = j // UPC, j % UPC, UPC, 0, hT_hi, hT_lo
                    else:
                        g, jj, n_units = 2 + (j - 2 * UPC) // UPO, (j - 2 * UPC) % UPO, UPO
                        k_off, hi, lo = 8 * (g - 2), yT_hi, yT_lo
                        if isinstance(i, int) and jj == 0:
                            t_left(pe, T_INDEX[("y", SWA_HEADS // 2 - 1 if g == 2 else SWA_HEADS // 2 + FOX_HEADS - 1)])
                    if jj == 0:
                        group_start((G_MIX + g) % 2, i * 2 + (G_MIX + g) // 2)
                    unit(u + j, j % RING, acc[(G_MIX + g) % 2], hi, lo, k_off + UK * jj, jj == 0, jj == n_units - 1)
                    if isinstance(i, int):
                        after(u + j)
                    elif j == 1:
                        merged_transposes(i - 1)

            mix(0)
            with pe.Fori(1, NC) as i:
                mix(i)
            for n in range(E0):
                group_start((G_E0 + n) % 2, (G_E0 + n) // 2)
                unit(U_E0 + n, (U_E0 + n) % RING, acc[(G_E0 + n) % 2], pT_hi, pT_lo, 0, True, True)
            merged_transposes(NC - 1)
            with pe.Fori(0, NC // 2) as i:
                for half in range(2):
                    u = i * (2 * UPC) + (U_OUT + half * UPC)
                    g = G_OUT + half
                    group_start(g % 2, i + g // 2)
                    for j in range(UPC):
                        if half == 0 and j == UPC - 2:
                            for n in (T_XN - 2, T_XN - 1):
                                t_left(pe, n)
                        unit(u + j, (U_OUT + j) % RING, acc[g % 2], mT_hi, mT_lo, UK * j, j == 0, j == UPC - 1)

            def x_new_transposes(j):
                i = T_XN + j
                pe.wait_ge(xn_ready, j + 1)
                pe.wait_ge(t_out[i % 2], i // 2)
                for k in range(2):
                    for t in range(NT):
                        r_ = pe.transpose(t_bank(i)[:, (2 * k + t) * P:(2 * k + t + 1) * P],
                                          x_new[:, t, (2 * j + k) * P:(2 * j + k + 1) * P], ident[:, :])
                r_.then_inc(t_done, 1)

            for n in range(E1):
                group_start((G_E1 + n) % 2, (G_E1 + n) // 2)
                unit(U_E1 + n, (U_E1 + n) % RING, acc[(G_E1 + n) % 2], pT_hi, pT_lo, 0, True, True)
            x_new_transposes(0)
            x_new_transposes(1)
            group_start(G_GATE % 2, G_GATE // 2)
            for j in range(UPC):
                t_left(pe, T_XN + j)
                unit(U_GATE + j, j % RING, acc[G_GATE % 2], hT_hi, hT_lo, UK * j, j == 0, j == UPC - 1)
                if j + 2 < UPC:
                    x_new_transposes(j + 2)
            for n in range(1, NC):
                g = G_GATE + n
                group_start(g % 2, g // 2)
                for j in range(UPC):
                    unit(U_GATE + n * UPC + j, j % RING, acc[g % 2], hT_hi, hT_lo, UK * j, j == 0, j == UPC - 1)


XN_AT = {U_GATE - 1: (0, 1)}
for _j in range(2, UPC):
    XN_AT[U_GATE + _j - 2] = (_j,)

_INS = ["x", "p", "positions", "pre_norm_g", "w_in", "b_forget", "sinks", "w_o_fox", "w_o_swa", "w_out",
        "post_norm_g", "w_ple", "w_ple_gate"]


def kernel(**inputs):
    import concourse.bacc as bacc
    from concourse.bass_utils import run_bass_kernel_spmd

    nc = bacc.Bacc("TRN2", target_bir_lowering=False, num_devices=1)
    arrays = {f"in_{n}": np.ascontiguousarray(inputs[n]) for n in _INS}
    for n in ("in_positions", "in_pre_norm_g"):
        arrays[n] = np.ascontiguousarray(arrays[n].reshape(-1, P).T)
    arrays["in_inv_freq"] = np.float32(ROPE_THETA) ** (-np.arange(HALF, dtype=np.float32) / np.float32(HALF))
    args = [nc.dram_tensor(n, a.shape, mybir.dt.from_np(a.dtype), kind="ExternalInput").ap() for n, a in arrays.items()]
    out = nc.dram_tensor("out_y", (1, SEQ, D_MODEL), F32, kind="ExternalOutput").ap()
    build(nc, *args, out)
    r = run_bass_kernel_spmd(nc, [arrays], core_ids=[0])
    return r.results[0]["out_y"]
```

```python
from contextlib import ExitStack

import numpy as np

import concourse.bass as bass
from concourse import mybir

F32 = mybir.dt.float32
F32R = mybir.dt.float32r
I32 = mybir.dt.int32
ACT = mybir.ActivationFunctionType
ALU = mybir.AluOpType
AX = mybir.AxisListType

P = 128
D_MODEL, SEQ = 2048, 256
FOX_HEADS, FOX_DIM = 8, 128
FOX_WIDTH = FOX_HEADS * FOX_DIM
SWA_HEADS, SWA_KV, SWA_DIM = 16, 2, 64
SWA_WIDTH = SWA_HEADS * SWA_DIM
KV_WIDTH = SWA_KV * SWA_DIM
GROUP = SWA_HEADS // SWA_KV
PLE_DIM = 256
EPS = 1e-6
ROPE_THETA = 10000.0
HALF = SWA_DIM // 2
MASKED = -1e30

NT = SEQ // P
KT = D_MODEL // P
N = 512
UK = 2
RING = 4
NC = D_MODEL // N
UPC = KT // UK
UPO = FOX_WIDTH // P // UK

_SIZES = (FOX_WIDTH,) * 4 + (FOX_HEADS, SWA_WIDTH, KV_WIDTH, KV_WIDTH, SWA_WIDTH, D_MODEL, D_MODEL)
C_QA, C_KA, C_VA, C_ZA, C_F, C_QB, C_KB, C_VB, C_ZB, C_GA, C_GB = np.cumsum((0,) + _SIZES[:-1]).tolist()
KVF = 2 * KV_WIDTH + FOX_HEADS

CHUNKS = [("kvf", 0, C_KB), ("qb", 0, C_QB), ("qb", 1, C_QB + N), ("zb", 0, C_ZB), ("zb", 1, C_ZB + N)]
for _g in range(2):
    CHUNKS += [("qa", _g, C_QA + _g * N), ("ka", _g, C_KA + _g * N),
               ("va", _g, C_VA + _g * N), ("za", _g, C_ZA + _g * N)]
NCH = len(CHUNKS)

U_MIX = NCH * UPC
MIX_UNITS = 2 * UPC + 2 * UPO
E0, E1 = 1, NC - 1
U_E0 = U_MIX + NC * MIX_UNITS
U_OUT = U_E0 + E0
U_E1 = U_OUT + NC * UPC
U_GATE = U_E1 + E1
U_END = U_GATE + NC * UPC
LAST_PIECES = ((0, slice(0, N)), (1, slice(0, N // 2)), (1, slice(N // 2, N)))
G_MIX = NCH
G_E0 = G_MIX + 4 * NC
G_OUT = G_E0 + E0
G_E1 = G_OUT + NC
E1_SIDE = 1
G_GATE = G_E1 + E1 - 1


def e1_group(n):
    return G_E1 + n - (n > E1_SIDE)

HEADS = SWA_HEADS + FOX_HEADS
SCORES_AT = [5 * UPC + 2 * h for h in range(SWA_HEADS)] + [72, 76, 80, 84, 101, 103, 105, 107]
HEAD_AT = {u: h for h, u in enumerate(SCORES_AT)}
KVF_OUT = UPC + 3
DECAY_AT = KVF_OUT + 5
BIAS_AT = DECAY_AT + 8

T_USES = [(17, "kbT", 0), (22, "qbT", 0), (23, "qbT", 1), (30, "qbT", 2), (31, "qbT", 3), (33, "pT", 0),
          (49, "qaT", 0), (50, "qaT", 1), (57, "kaT", 0), (58, "kaT", 1),
          (81, "qaT", 2), (82, "qaT", 3), (89, "kaT", 2), (90, "kaT", 3)]
T_USES += [(u + 2, "probs", h) for h, u in enumerate(SCORES_AT)]
T_USES += [(SCORES_AT[2 * q + 1] + 5, "y", q) for q in range(SWA_HEADS // 2)]
T_USES += [(SCORES_AT[SWA_HEADS + q] + 5, "y", SWA_HEADS // 2 + q) for q in range(FOX_HEADS)]
T_USES.sort(key=lambda use: use[0])
T_INDEX = {use[1:]: i for i, use in enumerate(T_USES)}
T_AT = {}
for _u in T_USES:
    T_AT.setdefault(_u[0], []).append(_u[1:])
T_MIX = len(T_USES)
T_XN = T_MIX + 2 * NC

X_AT = {0: (2,), 1: (3, 4), 2: (5,), 3: (6,), 4: (7,)}
X_BEFORE = {0: 0, 1: 1, 3: 2, 4: 3, 5: 4, 6: 5, 7: 6, 8: 7}

TWO_PI_1 = 6.28125
TWO_PI_2 = float(np.float32(np.float16(2 * np.pi - TWO_PI_1)))
TWO_PI_3 = float(np.float32(2 * np.pi - TWO_PI_1 - TWO_PI_2))
ROUND = 12582912.0
PI_BELOW = 3.1415925


def build(nc, x, p, positions, pre_norm_g, w_in, b_forget, sinks, w_o_fox, w_o_swa, w_out, post_norm_g,
          w_ple, w_ple_gate, inv_freq, out):
    ctx = ExitStack()

    def sb(name, shape, dt=F32, stack=ctx):
        return stack.enter_context(nc.sbuf_tensor(name, shape, dt))

    def sem(name):
        return ctx.enter_context(nc.semaphore(name))

    with ctx:
        w_st = sb("w_st", [P, RING, UK, N])
        w_hi = sb("w_hi", [P, RING, UK, N], F32R)
        w_lo = sb("w_lo", [P, RING, UK, N], F32R)
        hT_hi = sb("hT_hi", [P, KT, SEQ], F32R)
        hT_lo = sb("hT_lo", [P, KT, SEQ], F32R)
        ident = sb("ident", [P, P])
        pT_hi = sb("pT_hi", [P, 2, SEQ], F32R)
        pT_lo = sb("pT_lo", [P, 2, SEQ], F32R)
        g1T = sb("g1T", [P, KT])
        sumsq = sb("sumsq", [P, NT])
        rms = sb("rms", [P, 5, NT])
        half = sb("half", [P, NT])
        sumsq2 = sb("sumsq2", [P, NC, NT])
        rms2 = sb("rms2", [P, 3, NT])

        with ExitStack() as early:
            x_in = sb("x_in", [P, NT, D_MODEL], stack=early)
            p_in = sb("p_in", [P, NT, PLE_DIM], stack=early)
            w_f = sb("w_f", [P, KT, FOX_HEADS], stack=early)
        with ExitStack() as late:
            x_res = sb("x_res", [P, NT, D_MODEL], stack=late)
            x_new = sb("x_new", [P, NT, D_MODEL], stack=late)
        yT_hi = sb("yT_hi", [P, 16, SEQ], F32R)
        yT_lo = sb("yT_lo", [P, 16, SEQ], F32R)

        with ExitStack() as att:
            qaT = sb("qaT", [P, FOX_HEADS, SEQ], stack=att)
            kaT = sb("kaT", [P, FOX_HEADS, SEQ], stack=att)
            qbT = sb("qbT", [P, SWA_HEADS // 2, SEQ], stack=att)
            kbT = sb("kbT", [P, SWA_KV, SEQ], stack=att)
            va = sb("va", [P, NT, FOX_WIDTH], stack=att)
            vb = sb("vb", [P, NT, KV_WIDTH], stack=att)
            sza = sb("sza", [P, NT, FOX_WIDTH], stack=att)
            szb = sb("szb", [P, NT, SWA_WIDTH], stack=att)
            bias = sb("bias", [P, FOX_HEADS, 3 * P], stack=att)
            mask = sb("mask", [P, 2, 3 * P], stack=att)
            tri = sb("tri", [P, 3 * P], stack=att)
            probs = sb("probs", [P, 2, 3 * P], stack=att)
            probsT = sb("probsT", [P, 2, 3 * P], stack=att)
            ybuf = sb("ybuf", [P, 2, NT, P], stack=att)
            raw = sb("raw", [P, NT, N], stack=att)
            rot = sb("rot", [P, NT, N], stack=att)
            rtmp = sb("rtmp", [P, NT, N], stack=att)
            trig = sb("trig", [P, 3, NT, HALF], stack=att)
            turn = sb("turn", [P, 2, NT, HALF], stack=att)
            ang = sb("ang", [P, 2, NT, HALF], stack=att)
            inv_sb = sb("inv_sb", [P, HALF], stack=att)
            pos_i = sb("pos_i", [P, NT], I32, stack=att)
            pos_f = sb("pos_f", [P, NT], stack=att)
            bf_sb = sb("bf_sb", [P, FOX_HEADS], stack=att)
            sink_sb = sb("sink_sb", [P, SWA_HEADS], stack=att)
            fg = sb("fg", [P, 4, NT, FOX_HEADS], stack=att)
            log_f = sb("log_f", [P, NT, FOX_HEADS], stack=att)
            row = sb("row", [P, 6, HEADS, NT], stack=att)
        sg = sb("sg", [P, 2, NT, N])
        mT_hi = sb("mT_hi", [P, KT, SEQ], F32R)
        mT_lo = sb("mT_lo", [P, KT, SEQ], F32R)
        ple = sb("ple", [P, NT, D_MODEL])
        g2_sb = sb("g2_sb", [P, D_MODEL])

        decay_rows = probsT[0:FOX_HEADS, 0, :]

        acc = [ctx.enter_context(nc.psum_tensor(f"acc{i}", [P, NT, N], F32)) for i in range(2)]
        tp = [ctx.enter_context(nc.psum_tensor(f"tp{i}", [P, N], F32)) for i in range(2)]
        sc = ctx.enter_context(nc.psum_tensor("sc", [P, N], F32))
        ov = ctx.enter_context(nc.psum_tensor("ov", [P, N], F32))

        def banks_of(g):
            return [acc[g % 2][:, t, :] for t in range(NT)]

        last_acc = acc[(G_GATE + NC - 1) % 2]
        last_bank = [last_acc[:, 0, :], last_acc[:, 1, 0:N // 2], sc[:, 0:N // 2]]
        four = [tp[0], tp[1], sc, ov]

        w_loaded = [sem(f"w_loaded{i}") for i in range(RING)]
        f_loaded = sem("f_loaded")
        hi_ready, lo_ready, unit_done = sem("hi_ready"), sem("lo_ready"), sem("unit_done")
        acc_out = [sem("acc_out0"), sem("acc_out1")]
        t_done = sem("t_done")
        t_out = [sem("t_out0"), sem("t_out1")]
        x_loaded = [sem(f"x_loaded{i}") for i in range(UPC)]
        g1_loaded, pos_loaded, small_loaded, p_loaded = sem("g1_loaded"), sem("pos_loaded"), sem("small_loaded"), sem("p_loaded")
        late_loaded = [sem("x_res_loaded"), sem("g2_loaded")]
        ident_ready, masks_ready, const_ready = sem("ident_ready"), sem("masks_ready"), sem("const_ready")
        xT_done, hT_hi_ready, hT_ready = sem("xT_done"), sem("hT_hi_ready"), sem("hT_ready")
        sumsq_ready, ms_ready, pow_ready, r_ready = sem("sumsq_ready"), sem("ms_ready"), sem("pow_ready"), sem("r_ready")
        angle_step, angle_ready, trig_ready, nsin_ready = sem("angle_step"), sem("angle_ready"), sem("trig_ready"), sem("nsin_ready")
        k_raw, rope_step, rope_done = sem("k_raw"), sem("rope_step"), sem("rope_done")
        f_step, f_exp, f_one, f_ln, log_f_ready = sem("f_step"), sem("f_exp"), sem("f_one"), sem("f_ln"), sem("log_f_ready")
        decay_done, decay_copied, decay_stored = sem("decay_done"), sem("decay_copied"), sem("decay_stored")
        decay_spread, bias_ready = sem("decay_spread"), sem("bias_ready")
        hi_part = sem("hi_part")
        vb_ready = sem("vb_ready")
        z_tanh = sem("z_tanh")
        scores_done, row_max, neg_max, exp_done = sem("scores_done"), sem("row_max"), sem("neg_max"), sem("exp_done")
        den_ready, rec_ready, inv_ready = sem("den_ready"), sem("rec_ready"), sem("inv_ready")
        pv_done, y_ready = sem("pv_done"), sem("y_ready")
        merged_ready = sem("merged_ready")
        sq_ready = sem("sq_ready")
        ms2_step, pow2_ready, xn_ready = sem("ms2_step"), sem("pow2_ready"), sem("xn_ready")
        gate_step, result_ready = sem("gate_step"), sem("result_ready")
        piece_done, piece_tanh = sem("piece_done"), sem("piece_tanh")
        side_out = sem("side_out")
        stored = [sem("stored0"), sem("stored1")]

        decay_dram = nc.dram_tensor("decay_dram", (FOX_HEADS, 3 * P), F32, kind="Internal").ap()
        x_v = x.rearrange("b (t p) d -> p (b t) d", p=P)
        out_v = out.rearrange("b (t p) d -> p (b t) d", p=P)
        w_in_v = w_in.rearrange("a (k p) n -> p (a k) n", p=P)
        fox_v = w_o_fox.rearrange("a (k p) n -> p (a k) n", p=P)
        swa_v = w_o_swa.rearrange("a (k p) n -> p (a k) n", p=P)
        out_w = w_out.rearrange("a (k p) n -> p (a k) n", p=P)
        ple_w = w_ple.rearrange("a (k p) n -> p (a k) n", p=P)
        gate_w = w_ple_gate.rearrange("a (k p) n -> p (a k) n", p=P)

        def width(u):
            return KVF if isinstance(u, int) and u < UPC else N

        def t_bank(i):
            return tp[i % 2]

        def left(eng, g):
            eng.wait_ge(acc_out[g % 2], g // 2 + 1)

        def t_left(eng, i):
            eng.wait_ge(t_out[i % 2], i // 2 + 1)

        half_ready, exponents_ready = sem("half_ready"), sem("exponents_ready")

        block = ctx.enter_context(nc.Block())

        @block.sync
        def _(sp):
            def load(u, slot, view, k, cols):
                count = sp.lower_val(u - RING + 1)
                dma = sp.dma_start(w_st[:, slot, :, :], view[:, k:k + UK, cols])
                dma.wait_op(lo_ready, count, "sem-ge")
                dma.then_inc(w_loaded[slot], 16)

            for u in range(UPC):
                cols = slice(u * UK * P, (u + 1) * UK * P)
                sp.dma_start(x_in[:, :, cols], x_v[:, :, cols]).then_inc(x_loaded[u], 16)
                if u == 1:
                    sp.dma_start(w_f[:, :, :], w_in_v[:, :, C_F:C_F + FOX_HEADS]).then_inc(f_loaded, 16)
                if u >= RING:
                    sp.wait_ge(lo_ready, u - RING + 1)
                s, k = u % RING, UK * u
                sp.dma_start(w_st[:, s, :, 0:2 * KV_WIDTH],
                             w_in_v[:, k:k + UK, C_KB:C_KB + 2 * KV_WIDTH]).then_inc(w_loaded[s], 16)
            for c in range(1, NCH):
                for j in range(UPC):
                    load(c * UPC + j, j % RING, w_in_v, UK * j, slice(CHUNKS[c][2], CHUNKS[c][2] + N))
            with sp.Fori(0, NC) as i:
                u = i * MIX_UNITS + U_MIX
                for j in range(UPC):
                    load(u + j, j % RING, w_in_v, UK * j, bass.ds(i * N + C_GA, N))
                for j in range(UPC):
                    load(u + (UPC + j), j % RING, w_in_v, UK * j, bass.ds(i * N + C_GB, N))
                for j in range(UPO):
                    load(u + (2 * UPC + j), j % RING, swa_v, UK * j, bass.ds(i * N, N))
                for j in range(UPO):
                    load(u + (2 * UPC + UPO + j), j % RING, fox_v, UK * j, bass.ds(i * N, N))
            for n in range(E0):
                load(U_E0 + n, (U_E0 + n) % RING, ple_w, 0, slice(n * N, (n + 1) * N))
            with sp.Fori(0, NC) as i:
                u = i * UPC + U_OUT
                for j in range(UPC):
                    load(u + j, (U_OUT + j) % RING, out_w, UK * j, bass.ds(i * N, N))
                    if j == UPC - 2:
                        sp.dma_start(x_res[:, :, bass.ds(i * N, N)], x_v[:, :, bass.ds(i * N, N)]).then_inc(late_loaded[0], 16)
                        sp.dma_start(g2_sb[:, bass.ds(i * N, N)],
                                     post_norm_g[0, bass.ds(i * N, N)].partition_broadcast(P)).then_inc(late_loaded[1], 16)
            for n in range(E1):
                load(U_E1 + n, (U_E1 + n) % RING, ple_w, 0, slice((E0 + n) * N, (E0 + n + 1) * N))
            with sp.Fori(0, NC) as i:
                u = i * UPC + U_GATE
                for j in range(UPC):
                    load(u + j, j % RING, gate_w, UK * j, bass.ds(i * N, N))
            n = NC - 1
            for i, (t, cols) in enumerate(LAST_PIECES):
                sp.wait_ge(result_ready, n + i + 1)
                sp.dma_start(out_v[:, t, n * N + cols.start:n * N + cols.stop], sg[:, n % 2, t, cols]).then_inc(stored[n % 2], 16)
            sp.wait_ge(stored[0], 16 * (NC // 2))
            sp.wait_ge(stored[1], 16 * (NC // 2 - 1 + len(LAST_PIECES)))

        @block.gpsimd
        def _(pool):
            pool.memset(ident[:, :], 0.0).then_inc(const_ready, 1)
            pool.wait_ge(const_ready, 1)
            pool.affine_select(out=ident[:, :], in_=ident[:, :], compare_op=ALU.not_equal, fill=1.0,
                               base=0, pattern=[[-1, P]], channel_multiplier=1).then_inc(ident_ready, 1)

            pool.dma_start(pos_i[:, :], positions).then_inc(pos_loaded, 16)
            pool.dma_start(inv_sb[:, :], inv_freq.partition_broadcast(P)).then_inc(pos_loaded, 16)
            pool.dma_start(bf_sb[:, :], b_forget[0].partition_broadcast(P)).then_inc(small_loaded, 16)
            pool.dma_start(sink_sb[:, :], sinks[0].partition_broadcast(P)).then_inc(small_loaded, 16)
            pool.memset(mask[:, :, :], 0.0)
            pool.memset(tri[:, :], -1.0).then_inc(const_ready, 1)
            pool.wait_ge(const_ready, 2)
            for m in range(2):
                for b in (0, 2):
                    v = mask[:, m, b * P:(b + 1) * P]
                    pool.affine_select(out=v, in_=v, compare_op=ALU.is_ge, fill=MASKED, base=0,
                                       pattern=[[-1, P]], channel_multiplier=1).then_inc(masks_ready, 1)
            v = mask[:, 1, P:2 * P]
            pool.affine_select(out=v, in_=v, compare_op=ALU.is_gt, fill=MASKED, base=0,
                               pattern=[[1, P]], channel_multiplier=-1).then_inc(masks_ready, 1)
            for b in range(2):
                v = tri[:, b * P:(b + 1) * P]
                pool.affine_select(out=v, in_=v, compare_op=ALU.is_ge, fill=0.0, base=0,
                                   pattern=[[1, P]], channel_multiplier=-1).then_inc(masks_ready, 1)
            pool.dma_start(p_in[:, :, :], p.rearrange("a b (t p) d -> p (a b t) d", p=P)).then_inc(p_loaded, 16)
            pool.wait_ge(exponents_ready, 1)
            pool.wait_ge(ms_ready, 1)
            pool.tensor_tensor(rms[:, 2, :], rms[:, 0, :], rms[:, 1, :], ALU.pow).then_inc(pow_ready, 1)
            pool.wait_ge(nsin_ready, 1)
            steps = 0
            for c in range(3):
                heads = SWA_KV if c == 0 else N // SWA_DIM
                w = heads * SWA_DIM
                if c == 0:
                    pool.wait_ge(k_raw, 1)
                else:
                    left(pool, c)
                if c:
                    pool.wait_ge(t_done, T_INDEX[("kbT", 0) if c == 1 else ("qbT", 1)] + 1)
                src = raw[:, :, 0:w].rearrange("p t (h a d) -> p t h a d", a=2, d=HALF)
                for t in range(NT):
                    pool.tensor_tensor(rtmp[:, t, 0:w].rearrange("p (h d) -> p h d", d=HALF),
                                       raw[:, t, 0:w].rearrange("p (h d) -> p h d", d=HALF),
                                       trig[:, 1:2, t, :].to_broadcast([P, 2 * heads, HALF]), ALU.mult)
                off = 0 if c else 2 * w
                crossed = rot[:, :, off:off + w].rearrange("p t (h a d) -> p t h a d", a=2, d=HALF)
                for t in range(NT):
                    for a in range(2):
                        r_ = pool.tensor_tensor(
                            crossed[:, t, :, a, :], src[:, t, :, 1 - a, :],
                            trig[:, 2 * (1 - a):2 * (1 - a) + 1, t, :].to_broadcast([P, heads, HALF]), ALU.mult)
                r_.then_inc(rope_step, 1)
                steps += 1
                pool.wait_ge(rope_step, steps)
                if c:
                    pool.tensor_tensor(rot[:, :, :], rtmp[:, :, :], rot[:, :, :], ALU.add).then_inc(rope_done, 1)
                else:
                    for kv in range(SWA_KV):
                        for dup in range(2):
                            r_ = pool.tensor_tensor(
                                rot[:, :, (2 * kv + dup) * SWA_DIM:(2 * kv + dup + 1) * SWA_DIM],
                                rtmp[:, :, kv * SWA_DIM:(kv + 1) * SWA_DIM],
                                rot[:, :, 2 * w + kv * SWA_DIM:2 * w + (kv + 1) * SWA_DIM], ALU.add)
                    r_.then_inc(rope_done, 1)
            pool.wait_ge(ms2_step, 2)
            pool.tensor_tensor(rms2[:, 2, :], rms2[:, 0, :], rms2[:, 1, :], ALU.pow).then_inc(pow2_ready, 1)

        @block.scalar
        def _(act):
            act.dma_start(g1T[:, :], pre_norm_g).then_inc(g1_loaded, 16)
            act.wait_ge(half_ready, 1)
            act.activation(rms[:, 1, :], half[:, :], ACT.Copy, scale=-1.0)
            act.activation(rms2[:, 1, :], half[:, :], ACT.Copy, scale=-1.0).then_inc(exponents_ready, 1)

            def w_high(u, slot, turn_):
                act.wait_ge(w_loaded[slot], turn_ * 16 + 16)
                if not isinstance(u, int) or u >= RING:
                    act.wait_ge(unit_done, u - RING + 1)
                w = N
                if width(u) == KVF:
                    w = 2 * KV_WIDTH
                r_ = act.activation(w_hi[:, slot, :, 0:w], w_st[:, slot, :, 0:w], ACT.Copy)
                if width(u) == KVF:
                    act.wait_ge(f_loaded, 16)
                    r_ = act.activation(w_hi[:, slot, :, w:KVF], w_f[:, UK * u:UK * (u + 1), :], ACT.Copy)
                r_.then_inc(hi_ready, 1)

            def x_high(j):
                act.wait_ge(xT_done, j + 1)
                for k in range(2):
                    r_ = act.activation(hT_hi[:, 2 * j + k, :], four[j % 4][:, k * SEQ:(k + 1) * SEQ], ACT.Copy,
                                        scale=g1T[:, 2 * j + k:2 * j + k + 1])
                r_.then_inc(hT_hi_ready, 1)

            def evacuate(c):
                what, g, _ = CHUNKS[c]
                a = acc[c % 2]
                act.wait_ge(unit_done, UPC * (c + 1))
                if what == "kvf":
                    act.wait_ge(r_ready, 1)
                    for dst, cols, ready in ((raw[:, :, 0:KV_WIDTH], slice(0, KV_WIDTH), k_raw),
                                             (vb, slice(KV_WIDTH, 2 * KV_WIDTH), vb_ready),
                                             (fg[:, 0, :, :], slice(2 * KV_WIDTH, KVF), acc_out[0])):
                        for t in range(NT):
                            r_ = act.activation(dst[:, t, :], a[:, t, cols], ACT.Copy, scale=rms[:, 2, t:t + 1])
                        r_.then_inc(ready, 1)
                elif what in ("qb", "qa", "ka"):
                    if what == "qb" and g == 0:
                        act.wait_ge(rope_done, 1)
                    if what == "qb" and g == 1:
                        act.wait_ge(rope_done, 2)
                    if what == "qa" and g == 0:
                        act.wait_ge(rope_done, 3)
                    which = 4 if what == "qa" else 2
                    for t in range(NT):
                        r_ = act.activation(raw[:, t, :], a[:, t, :], ACT.Copy, scale=rms[:, which, t:t + 1])
                    r_.then_inc(acc_out[c % 2], 1)
                elif what == "va":
                    for t in range(NT):
                        r_ = act.activation(va[:, t, g * N:(g + 1) * N], a[:, t, :], ACT.Copy, scale=rms[:, 2, t:t + 1])
                    r_.then_inc(acc_out[c % 2], 1)
                else:
                    dst = szb if what == "zb" else sza
                    act.wait_ge(sumsq_ready, 2)
                    for t in range(NT):
                        r_ = act.activation(dst[:, t, g * N:(g + 1) * N], a[:, t, :], ACT.Tanh, scale=rms[:, 3, t:t + 1])
                    r_.then_inc(z_tanh, 1)

            def exps(h):
                act.wait_ge(neg_max, h + 1)
                b = probs[:, h % 2, :]
                for t, cols in ((0, slice(0, P)), (1, slice(P, 3 * P))):
                    r_ = act.activation(b[:, cols], b[:, cols], ACT.Exp, bias=row[:, 1, h, t:t + 1],
                                        accum_out=row[:, 2, h, t:t + 1])
                if h < SWA_HEADS:
                    r_ = act.activation(row[:, 3, h, :], row[:, 1, h, :], ACT.Exp, bias=sink_sb[:, h:h + 1])
                r_.then_inc(exp_done, 1)

            def copy_out(what, n):
                i = T_INDEX[(what, n)]
                act.wait_ge(t_done, i + 1)
                src = t_bank(i)
                if what == "probs":
                    if n >= 2:
                        act.wait_ge(pv_done, n - 1)
                    act.activation(probsT[:, n % 2, :], src[:, 0:3 * P], ACT.Copy).then_inc(t_out[i % 2], 1)
                elif what in ("y", "pT"):
                    w = 2 * SEQ if what == "pT" else SEQ
                    dst = pT_hi[:, :, :] if what == "pT" else yT_hi[:, n:n + 1, :]
                    act.activation(dst, src[:, 0:w].rearrange("p (k s) -> p k s", s=SEQ), ACT.Copy).then_inc(hi_part, 1)
                else:
                    dst = {"kbT": kbT, "qbT": qbT, "qaT": qaT, "kaT": kaT}[what]
                    scale = SWA_DIM ** -0.5 if what == "qbT" else 1.0
                    act.activation(dst[:, 2 * n:2 * n + 2, :], src[:, :].rearrange("p (k s) -> p k s", s=SEQ),
                                   ACT.Copy, scale=scale).then_inc(t_out[i % 2], 1)

            def after(u):
                if u == UPC - 1:
                    act.wait_ge(angle_ready, 1)
                    act.activation(trig[:, 0:2, :, :], ang[:, :, :, :], ACT.Sin).then_inc(trig_ready, 1)
                if u in (UPC, UPC + 1):
                    t = u - UPC
                    for x_part in x_loaded:
                        act.wait_ge(x_part, 16)
                    act.activation((sza, szb)[t][:, :, :], x_in[:, t, :].rearrange("p (a n) -> p a n", a=NT), ACT.Square,
                                   accum_out=sumsq[:, t:t + 1]).then_inc(sumsq_ready, 1)
                if u == KVF_OUT or u % UPC == UPC - 1 and UPC < u < U_MIX:
                    evacuate(0 if u == KVF_OUT else u // UPC)
                if u == KVF_OUT + 1:
                    act.wait_ge(f_step, 3)
                    act.activation(fg[:, 2, :, :], fg[:, 1, :, :], ACT.Exp, scale=-1.0).then_inc(f_exp, 1)
                if u == KVF_OUT + 2:
                    act.wait_ge(f_one, 1)
                    act.activation(fg[:, 3, :, :], fg[:, 2, :, :], ACT.Ln).then_inc(f_ln, 1)
                if u == DECAY_AT:
                    act.wait_ge(decay_done, 1)
                    act.activation(decay_rows, sc[0:FOX_HEADS, 0:3 * P], ACT.Copy).then_inc(decay_copied, 1)
                if u == DECAY_AT + 1:
                    act.wait_ge(decay_copied, 1)
                    act.dma_start(decay_dram[:, :], decay_rows).then_inc(decay_stored, 16)
                if u == DECAY_AT + 3:
                    act.wait_ge(decay_stored, 16)
                    act.dma_start(bias[:, :, :], decay_dram.partition_broadcast(P)).then_inc(decay_spread, 16)
                if u - 1 in HEAD_AT:
                    exps(HEAD_AT[u - 1])
                for use in T_AT.get(u, ()):
                    copy_out(*use)

            def gate_tanh(slot_g):
                for t in range(NT):
                    r_ = act.activation(sg[:, slot_g, t, :], acc[(G_MIX + slot_g) % 2][:, t, :], ACT.Tanh,
                                        scale=rms[:, 3, t:t + 1])
                r_.then_inc(acc_out[(G_MIX + slot_g) % 2], 1)

            def merged_high(i, s):
                n = T_MIX + s
                act.wait_ge(t_done, i * 2 + (n + 1))
                act.activation(mT_hi[:, bass.ds(i * 4 + 2 * s, 2), :], t_bank(n)[:, :].rearrange("p (k s) -> p k s", s=SEQ), ACT.Copy, scale=0.5).then_inc(hi_part, 1)

            def mix(i):
                u = i * MIX_UNITS + U_MIX
                turn_ = i * (MIX_UNITS // RING) + (U_MIX // RING)
                for j in range(MIX_UNITS):
                    w_high(u + (j + RING), j % RING, turn_ + (j // RING + 1))
                    if isinstance(i, int):
                        after(u + j)
                    if not isinstance(i, int) and j == 1:
                        for s in range(2):
                            merged_high(i - 1, s)
                    if j in (UPC - 1, 2 * UPC - 1):
                        which = j // UPC
                        act.wait_ge(unit_done, u + (j + 1))
                        gate_tanh(which)

            for u in range(RING):
                if u == 0:
                    act.wait_ge(g1_loaded, 16)
                if u in X_BEFORE:
                    x_high(X_BEFORE[u])
                w_high(u, u, 0)
            for u in range(U_MIX):
                if u + RING in X_BEFORE:
                    x_high(X_BEFORE[u + RING])
                w_high(u + RING, u % RING, u // RING + 1)
                after(u)
            mix(0)
            with act.Fori(1, NC) as i:
                mix(i)

            def last_tanh(n):
                g = G_GATE + n
                act.wait_ge(unit_done, U_GATE + UPC * (n + 1))
                if n >= 2:
                    act.wait_ge(stored[n % 2], 16 * (n // 2))
                act.activation(sg[:, n % 2, :, :], acc[g % 2][:, :, :], ACT.Tanh, scale=0.5).then_inc(acc_out[g % 2], 1)

            def last_tanh_pieces():
                n = NC - 1
                act.wait_ge(stored[n % 2], 16 * (n // 2))
                for i, (t, cols) in enumerate(LAST_PIECES):
                    act.wait_ge(piece_done, i + 1)
                    act.activation(sg[:, n % 2, t, cols], last_bank[i], ACT.Tanh,
                                   scale=0.5).then_inc(piece_tanh, 1)

            def squares(n):
                act.wait_ge(unit_done, U_OUT + UPC * (n + 1))
                for t in range(NT):
                    act.activation(sg[:, 0, t, :], acc[(G_OUT + n) % 2][:, t, :], ACT.Square,
                                   accum_out=sumsq2[:, n, t:t + 1]).then_inc(sq_ready, 1)

            for u in range(U_E0, U_END):
                if u == U_E1 - 1:
                    squares(NC - 1)
                if U_GATE - 2 <= u < U_GATE + UPC - 2:
                    j = u - U_GATE + 2
                    i = T_XN + j
                    act.wait_ge(t_done, i + 1)
                    act.activation(hT_hi[:, 2 * j:2 * j + 2, :], t_bank(i)[:, :].rearrange("p (k s) -> p k s", s=SEQ),
                                   ACT.Copy).then_inc(hi_part, 1)
                if u + RING < U_END:
                    w_high(u + RING, u % RING, u // RING + 1)
                if u < U_OUT or U_E1 <= u < U_GATE:
                    n = u - U_E0 if u < U_OUT else E0 + u - U_E1
                    g = G_E0 + n if n < E0 else e1_group(n - E0)
                    act.wait_ge(unit_done, u + 1)
                    if n == E0 + E1_SIDE:
                        for t, bank in enumerate((sc, ov)):
                            r_ = act.activation(ple[:, t, n * N:(n + 1) * N], bank[:, :], ACT.Copy, scale=0.5)
                        r_.then_inc(side_out, 1)
                    else:
                        act.activation(ple[:, :, n * N:(n + 1) * N], acc[g % 2][:, :, :], ACT.Copy, scale=0.5).then_inc(acc_out[g % 2], 1)
                if u == U_OUT - 1:
                    for s in range(2):
                        merged_high(NC - 1, s)
                if U_OUT <= u < U_E1 - 1 and (u - U_OUT) % UPC == UPC - 1:
                    squares((u - U_OUT) // UPC)
                if u >= U_GATE and (u - U_GATE) % UPC == UPC - 1 and u < U_END - 1:
                    last_tanh((u - U_GATE) // UPC)
                if u >= U_GATE + UPC and (u - U_GATE) % UPC == 1:
                    n = (u - U_GATE) // UPC - 1
                    act.wait_ge(result_ready, n + 1)
                    act.dma_start(out_v[:, :, n * N:(n + 1) * N], sg[:, n % 2, :, :]).then_inc(stored[n % 2], 16)
            last_tanh_pieces()

        @block.vector
        def _(dve):
            dve.memset(half[:, :], 0.5).then_inc(half_ready, 1)

            def angles():
                dve.wait_ge(pos_loaded, 32)
                dve.tensor_copy(pos_f[:, :], pos_i[:, :]).then_inc(angle_step, 1)
                dve.wait_ge(angle_step, 1)
                for t in range(NT):
                    for a in range(2):
                        r_ = dve.tensor_scalar(ang[:, a, t, :], inv_sb[:, :], pos_f[:, t:t + 1], None, ALU.mult)
                r_.then_inc(angle_step, 1)
                dve.wait_ge(angle_step, 2)
                for a in range(2):
                    r_ = dve.tensor_scalar(turn[:, a, :, :], ang[:, a, :, :], 1.0 / (2.0 * np.pi), 0.25 * a,
                                           ALU.mult, ALU.add)
                r_.then_inc(angle_step, 1)
                dve.wait_ge(angle_step, 3)
                dve.tensor_scalar(turn[:, :, :, :], turn[:, :, :, :], ROUND, -ROUND, ALU.add, ALU.add).then_inc(angle_step, 1)
                for n, part in enumerate((TWO_PI_1, TWO_PI_2, TWO_PI_3)):
                    dve.wait_ge(angle_step, 4 + n)
                    dve.scalar_tensor_tensor(out=ang[:, :, :, :], in0=turn[:, :, :, :], scalar=-part, in1=ang[:, :, :, :],
                                             op0=ALU.mult, op1=ALU.add).then_inc(angle_step, 1)
                dve.wait_ge(angle_step, 7)
                dve.tensor_scalar(ang[:, 1, :, :], ang[:, 1, :, :], 0.5 * np.pi, None, ALU.add).then_inc(angle_step, 1)
                dve.wait_ge(angle_step, 8)
                dve.tensor_scalar(ang[:, :, :, :], ang[:, :, :, :], PI_BELOW, -PI_BELOW, ALU.min, ALU.max).then_inc(angle_ready, 1)

            def w_low(u, slot):
                dve.wait_ge(hi_ready, u + 1)
                w = N
                if width(u) == KVF:
                    w = 2 * KV_WIDTH
                    dve.tensor_tensor(w_lo[:, slot, :, w:KVF], w_f[:, UK * u:UK * (u + 1), :],
                                      w_hi[:, slot, :, w:KVF].bitcast(F32), ALU.subtract)
                dve.tensor_tensor(w_lo[:, slot, :, 0:w], w_st[:, slot, :, 0:w], w_hi[:, slot, :, 0:w].bitcast(F32),
                                  ALU.subtract).then_inc(lo_ready, 1)

            def x_low(j):
                dve.wait_ge(hT_hi_ready, j + 1)
                for k in range(2):
                    kk = 2 * j + k
                    r_ = dve.scalar_tensor_tensor(out=hT_lo[:, kk, :], in0=four[j % 4][:, k * SEQ:(k + 1) * SEQ],
                                                  scalar=g1T[:, kk:kk + 1], in1=hT_hi[:, kk, :].bitcast(F32),
                                                  op0=ALU.mult, op1=ALU.subtract)
                r_.then_inc(hT_ready, 1)

            def split_low(dst_lo, dst_hi, n_hi, i, scale=1.0):
                dve.wait_ge(hi_part, n_hi)
                w = dst_hi.shape[1] * SEQ
                dve.scalar_tensor_tensor(out=dst_lo, in0=t_bank(i)[:, 0:w].rearrange("p (k s) -> p k s", s=SEQ), scalar=scale,
                                         in1=dst_hi.bitcast(F32), op0=ALU.mult, op1=ALU.subtract).then_inc(t_out[i % 2], 1)

            def silu(c):
                what, g, _ = CHUNKS[c]
                n = [i for i, x_ in enumerate(CHUNKS) if x_[0] in ("zb", "za")].index(c)
                v = (szb if what == "zb" else sza)[:, :, g * N:(g + 1) * N]
                dve.wait_ge(z_tanh, n + 1)
                dve.scalar_tensor_tensor(out=v, in0=v, scalar=1.0, in1=acc[c % 2][:, :, :], op0=ALU.add,
                                         op1=ALU.mult).then_inc(acc_out[c % 2], 1)

            def softmax_max(h):
                dve.wait_ge(scores_done, h + 1)
                if h >= 2:
                    dve.wait_ge(t_done, T_INDEX[("probs", h - 2)] + 1)
                b = mask[:, 1, :] if h < SWA_HEADS else bias[:, h - SWA_HEADS, :]
                for t, cols in ((0, slice(0, P)), (1, slice(P, 3 * P))):
                    r_ = dve.tensor_tensor_reduce(probs[:, h % 2, cols], sc[:, cols], b[:, cols], 1.0, -3e38, ALU.add,
                                                  ALU.max, row[:, 0, h, t:t + 1])
                r_.then_inc(row_max, 1)
                dve.wait_ge(row_max, h + 1)
                if h < SWA_HEADS:
                    dve.tensor_scalar(row[:, 1, h, :], row[:, 0, h, :], sink_sb[:, h:h + 1], -1.0, ALU.max,
                                      ALU.mult).then_inc(neg_max, 1)
                else:
                    dve.tensor_scalar(row[:, 1, h, :], row[:, 0, h, :], -1.0, None, ALU.mult).then_inc(neg_max, 1)

            def denominators(h):
                dve.wait_ge(exp_done, h + 1)
                which = 2
                if h < SWA_HEADS:
                    dve.tensor_tensor(row[:, 4, h, :], row[:, 2, h, :], row[:, 3, h, :], ALU.add).then_inc(den_ready, 1)
                    dve.wait_ge(den_ready, h + 1)
                    which = 4
                dve.reciprocal(row[:, 5, h, :], row[:, which, h, :]).then_inc(rec_ready, 1)
                dve.wait_ge(rec_ready, h + 1)
                dve.tensor_tensor(row[:, 5, h, :], row[:, 5, h, :], rms[:, 3, :], ALU.mult).then_inc(inv_ready, 1)

            def gated_values(h):
                fox = h >= SWA_HEADS
                q = SWA_HEADS // 2 + h - SWA_HEADS if fox else h // 2
                d = FOX_DIM if fox else SWA_DIM
                off = 0 if fox else (h % 2) * SWA_DIM
                zcol = ((h - SWA_HEADS) if fox else h) * d
                dve.wait_ge(pv_done, h + 1)
                dve.wait_ge(inv_ready, h + 1)
                left(dve, [c for c, x_ in enumerate(CHUNKS) if x_[0] == ("za" if fox else "zb")][zcol // N])
                if q >= 2 and off == 0:
                    dve.wait_ge(t_done, T_INDEX[("y", q - 2)] + 1)
                z = sza if fox else szb
                for t in range(NT):
                    r_ = dve.scalar_tensor_tensor(out=ybuf[:, q % 2, t, off:off + d], in0=ov[:, t * d:(t + 1) * d],
                                                  scalar=row[:, 5, h, t:t + 1], in1=z[:, t, zcol:zcol + d],
                                                  op0=ALU.mult, op1=ALU.mult)
                r_.then_inc(y_ready, 1)

            splits = [use[1:] for use in T_USES if use[1] in ("y", "pT")]

            def after(u):
                if u == UPC - 2:
                    angles()
                if u == UPC:
                    dve.wait_ge(trig_ready, 1)
                    dve.tensor_scalar(trig[:, 2, :, :], trig[:, 0, :, :], -1.0, None, ALU.mult).then_inc(nsin_ready, 1)
                if u == UPC + 1:
                    dve.wait_ge(sumsq_ready, 2)
                    dve.tensor_scalar(rms[:, 0, :], sumsq[:, :], 1.0 / D_MODEL, EPS, ALU.mult, ALU.add).then_inc(ms_ready, 1)
                if u == UPC + 2:
                    dve.wait_ge(pow_ready, 1)
                    dve.tensor_scalar(rms[:, 3, :], rms[:, 2, :], 0.5, None, ALU.mult)
                    dve.tensor_scalar(rms[:, 4, :], rms[:, 2, :], FOX_DIM ** -0.5, None, ALU.mult).then_inc(r_ready, 1)
                if u == KVF_OUT:
                    left(dve, 0)
                    dve.wait_ge(small_loaded, 32)
                    for t in range(NT):
                        r_ = dve.tensor_tensor(fg[:, 0, t, :], fg[:, 0, t, :], bf_sb[:, :], ALU.add)
                    r_.then_inc(f_step, 1)
                    dve.wait_ge(f_step, 1)
                    dve.tensor_scalar(fg[:, 1, :, :], fg[:, 0, :, :], -1.0, None, ALU.mult).then_inc(f_step, 1)
                    dve.wait_ge(f_step, 2)
                    dve.tensor_tensor(fg[:, 1, :, :], fg[:, 0, :, :], fg[:, 1, :, :], ALU.max).then_inc(f_step, 1)
                    dve.tensor_scalar(log_f[:, :, :], fg[:, 0, :, :], 0.0, None, ALU.min).then_inc(f_step, 1)
                if u == KVF_OUT + 1:
                    dve.wait_ge(f_exp, 1)
                    dve.tensor_scalar(fg[:, 2, :, :], fg[:, 2, :, :], 1.0, None, ALU.add).then_inc(f_one, 1)
                if u == KVF_OUT + 3:
                    dve.wait_ge(f_ln, 1)
                    dve.wait_ge(f_step, 4)
                    dve.tensor_tensor(log_f[:, :, :], log_f[:, :, :], fg[:, 3, :, :], ALU.subtract).then_inc(log_f_ready, 1)
                if u == BIAS_AT:
                    dve.wait_ge(decay_spread, 16)
                    dve.wait_ge(masks_ready, 7)
                    dve.tensor_tensor(bias[:, :, :], bias[:, :, :], mask[:, 0:1, :].to_broadcast([P, FOX_HEADS, 3 * P]),
                                      ALU.add).then_inc(bias_ready, 1)
                if u in HEAD_AT:
                    softmax_max(HEAD_AT[u])
                if u - 2 in HEAD_AT:
                    denominators(HEAD_AT[u - 2])
                if u - 3 in HEAD_AT:
                    gated_values(HEAD_AT[u - 3])
                for what, n in T_AT.get(u, ()):
                    if what in ("y", "pT"):
                        i = T_INDEX[(what, n)]
                        hi, lo = (pT_hi[:, :, :], pT_lo[:, :, :]) if what == "pT" else (yT_hi[:, n:n + 1, :], yT_lo[:, n:n + 1, :])
                        split_low(lo, hi, splits.index((what, n)) + 1, i)
                if u % UPC == UPC - 1 and u < U_MIX and CHUNKS[u // UPC][0] in ("zb", "za"):
                    silu(u // UPC)

            def merged_low(i, s):
                n = T_MIX + s
                if isinstance(i, int):
                    lo, hi = (m[:, 4 * i + 2 * s:4 * i + 2 * s + 2, :] for m in (mT_lo, mT_hi))
                else:
                    lo, hi = (m[:, bass.ds(i * 4 + 2 * s, 2), :] for m in (mT_lo, mT_hi))
                split_low(lo, hi, i * 2 + (len(splits) + s + 1), n, 0.5)

            def mix(i):
                u = i * MIX_UNITS + U_MIX
                for j in range(MIX_UNITS):
                    for g, last in ((1, 2 * UPC + UPO - 1), (0, MIX_UNITS - 1)):
                        if j == last:
                            n = (G_MIX + g) // 2 + 1
                            dve.wait_ge(unit_done, u + (j + 1))
                            dve.wait_ge(acc_out[(G_MIX + g) % 2], i * 2 + n)
                            bank = (G_MIX + 3 - g) % 2
                            dve.scalar_tensor_tensor(out=sg[:, g, :, :], in0=sg[:, g, :, :], scalar=1.0, in1=acc[bank][:, :, :],
                                                     op0=ALU.add, op1=ALU.mult).then_inc(acc_out[bank], 1)
                    if j == MIX_UNITS - 1:
                        for g in (2, 3):
                            dve.wait_ge(acc_out[(G_MIX + g) % 2], i * 2 + ((G_MIX + g) // 2 + 1))
                        for s in range(2):
                            part = slice(s * N // 2, (s + 1) * N // 2)
                            dve.tensor_tensor(sg[:, 0, :, part], sg[:, 0, :, part], sg[:, 1, :, part],
                                              ALU.add).then_inc(merged_ready, 1)
                    w_low(u + (j + RING), j % RING)
                    if isinstance(i, int):
                        after(u + j)
                    if not isinstance(i, int) and j == 1:
                        for s in range(2):
                            merged_low(i - 1, s)

            for u in range(RING):
                if u in X_BEFORE:
                    x_low(X_BEFORE[u])
                w_low(u, u)
            for u in range(U_MIX):
                if u + RING in X_BEFORE:
                    x_low(X_BEFORE[u + RING])
                w_low(u + RING, u % RING)
                after(u)
            mix(0)
            with dve.Fori(1, NC) as i:
                mix(i)

            def x_piece(j):
                cols = slice(2 * P * j, 2 * P * (j + 1))
                for t in range(NT):
                    r_ = dve.scalar_tensor_tensor(out=x_new[:, t, cols], in0=x_new[:, t, cols], scalar=rms2[:, 2, t:t + 1],
                                                  in1=x_res[:, t, cols], op0=ALU.mult, op1=ALU.add)
                r_.then_inc(xn_ready, 1)

            def times_g(n, t):
                dve.wait_ge(late_loaded[1], 16 * (n + 1))
                dve.wait_ge(sq_ready, NT * n + t + 1)
                r_ = dve.tensor_tensor(x_new[:, t, n * N:(n + 1) * N], acc[(G_OUT + n) % 2][:, t, :],
                                       g2_sb[:, n * N:(n + 1) * N], ALU.mult)
                if t == NT - 1:
                    r_.then_inc(acc_out[(G_OUT + n) % 2], 1)

            def first_of_x_new():
                dve.wait_ge(sq_ready, NT * NC)
                dve.tensor_reduce(rms2[:, 0, :], sumsq2[:, :, :].rearrange("p n t -> p t n"), AX.X, ALU.add).then_inc(ms2_step, 1)
                dve.wait_ge(ms2_step, 1)
                dve.tensor_scalar(rms2[:, 0, :], rms2[:, 0, :], 1.0 / D_MODEL, EPS, ALU.mult, ALU.add).then_inc(ms2_step, 1)
                times_g(NC - 1, 0)
                dve.wait_ge(pow2_ready, 1)
                dve.wait_ge(late_loaded[0], 16 * NC)
                for n in range(NC - 1):
                    left(dve, G_OUT + n)
                x_piece(0)
                times_g(NC - 1, 1)
                left(dve, G_OUT + NC - 1)
                x_piece(1)

            for u in range(U_E0, U_END):
                if u == U_E1 - 1:
                    first_of_x_new()
                if U_GATE - 2 <= u < U_GATE + UPC - 2:
                    j = u - U_GATE + 2
                    i = T_XN + j
                    split_low(hT_lo[:, 2 * j:2 * j + 2, :], hT_hi[:, 2 * j:2 * j + 2, :],
                              len(splits) + 2 * NC + j + 1, i)
                if u + RING < U_END:
                    w_low(u + RING, u % RING)
                if u == U_OUT - 1:
                    for s in range(2):
                        merged_low(NC - 1, s)
                if U_OUT <= u < U_E1 - 1 and (u - U_OUT) % UPC == UPC - 1:
                    for t in range(NT):
                        times_g((u - U_OUT) // UPC, t)
                if U_GATE - 3 <= u < U_GATE + UPC - 5:
                    x_piece(u - U_GATE + 5)
                if u >= U_GATE and (u - U_GATE) % UPC == UPC - 1 and u < U_END - 1:
                    n = (u - U_GATE) // UPC
                    cols = slice(n * N, (n + 1) * N)
                    v = sg[:, n % 2, :, :]
                    left(dve, G_GATE + n)
                    left(dve, G_GATE - 2)
                    left(dve, G_GATE - 1)
                    dve.wait_ge(side_out, 1)
                    dve.scalar_tensor_tensor(out=v, in0=v, scalar=1.0, in1=ple[:, :, cols], op0=ALU.add,
                                             op1=ALU.mult).then_inc(gate_step, 1)
                    dve.wait_ge(gate_step, n + 1)
                    dve.tensor_tensor(v, v, x_new[:, :, cols], ALU.add).then_inc(result_ready, 1)

            n = NC - 1
            for i, (t, cols) in enumerate(LAST_PIECES):
                v = sg[:, n % 2, t, cols]
                there = slice(n * N + cols.start, n * N + cols.stop)
                dve.wait_ge(piece_tanh, i + 1)
                dve.scalar_tensor_tensor(out=v, in0=v, scalar=1.0, in1=ple[:, t, there], op0=ALU.add,
                                         op1=ALU.mult).then_inc(gate_step, 1)
                dve.wait_ge(gate_step, n + i + 1)
                dve.tensor_tensor(v, v, x_new[:, t, there], ALU.add).then_inc(result_ready, 1)

        @block.tensor
        def _(pe):
            def x_transposes(j):
                if j >= 4:
                    pe.wait_ge(hT_ready, j - 3)
                pe.wait_ge(x_loaded[j], 16)
                for k in range(2):
                    for t in range(NT):
                        r_ = pe.transpose(four[j % 4][:, (2 * k + t) * P:(2 * k + t + 1) * P],
                                          x_in[:, t, (2 * j + k) * P:(2 * j + k + 1) * P], ident[:, :])
                r_.then_inc(xT_done, 1)

            def unit(u, slot, banks, lhs_hi, lhs_lo, k0, first, last, w=N):
                pe.wait_ge(lo_ready, u + 1)
                for k in range(UK):
                    for t in range(NT):
                        hi = lhs_hi[:, k0 + k, t * P:(t + 1) * P]
                        lo = lhs_lo[:, k0 + k, t * P:(t + 1) * P]
                        o = banks[t][:, 0:w]
                        pe.matmul(o, hi, w_hi[:, slot, k, 0:w], start=(first and k == 0), stop=False)
                        pe.matmul(o, hi, w_lo[:, slot, k, 0:w], start=False, stop=False)
                        r_ = pe.matmul(o, lo, w_hi[:, slot, k, 0:w], start=False, stop=(last and k == UK - 1))
                r_.then_inc(unit_done, 1)

            def transposes(what, n):
                i = T_INDEX[(what, n)]
                bank = t_bank(i)
                if i >= 2:
                    pe.wait_ge(t_out[i % 2], i // 2)
                if what == "probs":
                    pe.wait_ge(exp_done, n + 1)
                    src = [probs[:, n % 2, b * P:(b + 1) * P] for b in range(3)]
                elif what == "y":
                    pe.wait_ge(y_ready, 2 * n + 2 if n < SWA_HEADS // 2 else SWA_HEADS + n - SWA_HEADS // 2 + 1)
                    src = [ybuf[:, n % 2, t, :] for t in range(NT)]
                elif what == "pT":
                    pe.wait_ge(p_loaded, 16)
                    src = [p_in[:, t, k * P:(k + 1) * P] for k in range(2) for t in range(NT)]
                elif what in ("kbT", "qbT"):
                    pe.wait_ge(rope_done, 1 if what == "kbT" else 2 + n // 2)
                    src = [rot[:, t, (2 * (n % 2) + k) * P:(2 * (n % 2) + k + 1) * P] for k in range(2) for t in range(NT)]
                else:
                    left(pe, CHUNKS.index((what[0:2], n // 2, (C_QA if what == "qaT" else C_KA) + n // 2 * N)))
                    src = [raw[:, t, (2 * (n % 2) + k) * P:(2 * (n % 2) + k + 1) * P] for k in range(2) for t in range(NT)]
                for b, s in enumerate(src):
                    r_ = pe.transpose(bank[:, b * P:(b + 1) * P], s, ident[:, :])
                r_.then_inc(t_done, 1)

            def decay():
                pe.wait_ge(log_f_ready, 1)
                pe.wait_ge(masks_ready, 7)
                pe.matmul(sc[0:FOX_HEADS, 0:3 * P], log_f[:, 0, :], tri[:, :], start=True, stop=False)
                pe.matmul(sc[0:FOX_HEADS, 2 * P:3 * P], log_f[:, 1, :], tri[:, 0:P], start=False,
                          stop=True).then_inc(decay_done, 1)

            def scores(h):
                if h == 0:
                    pe.wait_ge(decay_copied, 1)
                    t_left(pe, T_INDEX[("qbT", 3)])
                    t_left(pe, T_INDEX[("qbT", 2)])
                    t_left(pe, T_INDEX[("kbT", 0)])
                else:
                    pe.wait_ge(row_max, h)
                if h < SWA_HEADS:
                    rows = slice((h % 2) * SWA_DIM, (h % 2 + 1) * SWA_DIM)
                    q, k = qbT[rows, h // 2, :], kbT[rows, h // GROUP, :]
                else:
                    f = h - SWA_HEADS
                    if f % 4 == 0:
                        for n in range(2):
                            t_left(pe, T_INDEX[("qaT", 2 * (f // 4) + n)])
                            t_left(pe, T_INDEX[("kaT", 2 * (f // 4) + n)])
                    q, k = qaT[:, f, :], kaT[:, f, :]
                pe.matmul(sc[:, 0:P], q[:, 0:P], k[:, 0:P], start=True, stop=True)
                pe.matmul(sc[:, P:3 * P], q[:, P:SEQ], k, start=True, stop=True).then_inc(scores_done, 1)

            def values(h):
                d = SWA_DIM if h < SWA_HEADS else FOX_DIM
                v, c = (vb, h // GROUP * d) if h < SWA_HEADS else (va, (h - SWA_HEADS) * d)
                t_left(pe, T_INDEX[("probs", h)])
                if h < SWA_HEADS:
                    pe.wait_ge(vb_ready, 1)
                else:
                    left(pe, [c_ for c_, x_ in enumerate(CHUNKS) if x_[0] == "va"][(h - SWA_HEADS) // 4])
                if h >= 1:
                    pe.wait_ge(y_ready, h)
                pT = probsT[:, h % 2, :]
                pe.matmul(ov[:, 0:d], pT[:, 0:P], v[:, 0, c:c + d], start=True, stop=True)
                pe.matmul(ov[:, d:2 * d], pT[:, P:2 * P], v[:, 0, c:c + d], start=True, stop=False)
                pe.matmul(ov[:, d:2 * d], pT[:, 2 * P:3 * P], v[:, 1, c:c + d], start=False, stop=True).then_inc(pv_done, 1)

            def after(u):
                for j in X_AT.get(u, ()):
                    x_transposes(j)
                if u == DECAY_AT:
                    decay()
                if u - 3 in HEAD_AT:
                    values(HEAD_AT[u - 3])
                if u in HEAD_AT:
                    scores(HEAD_AT[u])
                for use in T_AT.get(u, ()):
                    transposes(*use)

            def group_start(g_slot, uses):
                pe.wait_ge(acc_out[g_slot], uses)

            def warm_up(times):
                for _ in range(times):
                    pe.matmul(ov[:, 0:P], ident[:, :], ident[:, :], start=True, stop=True)

            pe.wait_ge(ident_ready, 1)
            for j in range(2):
                warm_up(4 - 2 * j)
                x_transposes(j)
            warm_up(2)
            for u in range(U_MIX):
                c, j = u // UPC, u % UPC
                if c == 0:
                    pe.wait_ge(hT_ready, j + 1)
                if j == 0 and c >= 2:
                    group_start(c % 2, c // 2)
                unit(u, u % RING, banks_of(c), hT_hi, hT_lo, UK * j, j == 0, j == UPC - 1, width(u))
                after(u)

            def merged_transposes(i):
                for s in range(2):
                    pe.wait_ge(merged_ready, i * 2 + (s + 1))
                    n = T_MIX + s
                    pe.wait_ge(t_out[n % 2], i + n // 2)
                    for k in range(2):
                        for t in range(NT):
                            r_ = pe.transpose(t_bank(n)[:, (2 * k + t) * P:(2 * k + t + 1) * P],
                                              sg[:, 0, t, (2 * s + k) * P:(2 * s + k + 1) * P], ident[:, :])
                    r_.then_inc(t_done, 1)

            def mix(i):
                u = i * MIX_UNITS + U_MIX
                for j in range(MIX_UNITS):
                    if j < 2 * UPC:
                        g, jj, n_units, k_off, hi, lo = j // UPC, j % UPC, UPC, 0, hT_hi, hT_lo
                    else:
                        g, jj, n_units = 2 + (j - 2 * UPC) // UPO, (j - 2 * UPC) % UPO, UPO
                        k_off, hi, lo = 8 * (g - 2), yT_hi, yT_lo
                        if isinstance(i, int) and jj == 0:
                            t_left(pe, T_INDEX[("y", SWA_HEADS // 2 - 1 if g == 2 else SWA_HEADS // 2 + FOX_HEADS - 1)])
                    if jj == 0:
                        group_start((G_MIX + g) % 2, i * 2 + (G_MIX + g) // 2)
                    unit(u + j, j % RING, banks_of(G_MIX + g), hi, lo, k_off + UK * jj, jj == 0, jj == n_units - 1)
                    if isinstance(i, int):
                        after(u + j)
                    elif j == 1:
                        merged_transposes(i - 1)

            mix(0)
            with pe.Fori(1, NC) as i:
                mix(i)
            for n in range(E0):
                group_start((G_E0 + n) % 2, (G_E0 + n) // 2)
                unit(U_E0 + n, (U_E0 + n) % RING, banks_of(G_E0 + n), pT_hi, pT_lo, 0, True, True)
            merged_transposes(NC - 1)
            with pe.Fori(0, NC // 2) as i:
                for odd in range(2):
                    u = i * (2 * UPC) + (U_OUT + odd * UPC)
                    g = G_OUT + odd
                    group_start(g % 2, i + g // 2)
                    for j in range(UPC):
                        if odd == 0 and j == UPC - 2:
                            for n in (T_XN - 2, T_XN - 1):
                                t_left(pe, n)
                        unit(u + j, (U_OUT + j) % RING, banks_of(g), mT_hi, mT_lo, UK * j, j == 0, j == UPC - 1)

            def x_new_transposes(j):
                i = T_XN + j
                pe.wait_ge(xn_ready, j + 1)
                pe.wait_ge(t_out[i % 2], i // 2)
                for k in range(2):
                    for t in range(NT):
                        r_ = pe.transpose(t_bank(i)[:, (2 * k + t) * P:(2 * k + t + 1) * P],
                                          x_new[:, t, (2 * j + k) * P:(2 * j + k + 1) * P], ident[:, :])
                r_.then_inc(t_done, 1)

            for n in range(E1):
                if n != E1_SIDE:
                    group_start(e1_group(n) % 2, e1_group(n) // 2)
                unit(U_E1 + n, (U_E1 + n) % RING, (sc, ov) if n == E1_SIDE else banks_of(e1_group(n)), pT_hi, pT_lo, 0, True, True)
                if U_E1 + n >= U_GATE - 2:
                    x_new_transposes(U_E1 + n - U_GATE + 2)
            group_start(G_GATE % 2, G_GATE // 2)
            for j in range(UPC):
                t_left(pe, T_XN + j)
                unit(U_GATE + j, j % RING, banks_of(G_GATE), hT_hi, hT_lo, UK * j, j == 0, j == UPC - 1)
                if j + 2 < UPC:
                    x_new_transposes(j + 2)
            for n in range(1, NC):
                g = G_GATE + n
                group_start(g % 2, g // 2)
                if n < NC - 1:
                    for j in range(UPC):
                        unit(U_GATE + n * UPC + j, j % RING, banks_of(g), hT_hi, hT_lo, UK * j, j == 0, j == UPC - 1)

            def piece_products(i, j):
                t, cols = LAST_PIECES[i]
                for k in range(UK):
                    hi = hT_hi[:, UK * j + k, t * P:(t + 1) * P]
                    lo = hT_lo[:, UK * j + k, t * P:(t + 1) * P]
                    last = j == UPC - 1 and k == UK - 1
                    pe.matmul(last_bank[i], hi, w_hi[:, j % RING, k, cols], start=(j == 0 and k == 0), stop=False)
                    pe.matmul(last_bank[i], hi, w_lo[:, j % RING, k, cols], start=False, stop=False)
                    r_ = pe.matmul(last_bank[i], lo, w_hi[:, j % RING, k, cols], start=False, stop=last)
                return r_

            pe.wait_ge(side_out, 1)
            for j in range(UPC - RING):
                pe.wait_ge(lo_ready, U_END - UPC + j + 1)
                for i in range(len(LAST_PIECES)):
                    r_ = piece_products(i, j)
                r_.then_inc(unit_done, 1)
            for i in range(len(LAST_PIECES)):
                for j in range(UPC - RING, UPC):
                    pe.wait_ge(lo_ready, U_END - UPC + j + 1)
                    r_ = piece_products(i, j)
                r_.then_inc(piece_done, 1)


_INS = ["x", "p", "positions", "pre_norm_g", "w_in", "b_forget", "sinks", "w_o_fox", "w_o_swa", "w_out",
        "post_norm_g", "w_ple", "w_ple_gate"]


def kernel(**inputs):
    import concourse.bacc as bacc
    from concourse.bass_utils import run_bass_kernel_spmd

    nc = bacc.Bacc("TRN2", target_bir_lowering=False, num_devices=1)
    arrays = {f"in_{n}": np.ascontiguousarray(inputs[n]) for n in _INS}
    for n in ("in_positions", "in_pre_norm_g"):
        arrays[n] = np.ascontiguousarray(arrays[n].reshape(-1, P).T)
    arrays["in_inv_freq"] = np.float32(ROPE_THETA) ** (-np.arange(HALF, dtype=np.float32) / np.float32(HALF))
    args = [nc.dram_tensor(n, a.shape, mybir.dt.from_np(a.dtype), kind="ExternalInput").ap() for n, a in arrays.items()]
    out = nc.dram_tensor("out_y", (1, SEQ, D_MODEL), F32, kind="ExternalOutput").ap()
    build(nc, *args, out)
    r = run_bass_kernel_spmd(nc, [arrays], core_ids=[0])
    return r.results[0]["out_y"]
```
